# Optimizing a Trainium2 kernel written in Bass

```python
import math
import jax, jax.numpy as jnp
from jax import lax
import numpy as np
import jax
import jax.numpy as jnp

D_MODEL = 1024
BATCH = 1
SEQ = 256
DEPTH = 2

N_EVEN = (DEPTH + 1) // 2
N_ODD = DEPTH // 2

A_QK_DIM = 64
A_V_DIM = 2 * A_QK_DIM
A_WIDTH = D_MODEL // 2
A_HEADS = A_WIDTH // A_V_DIM
ROPE_DIM = A_QK_DIM // 4
ROPE_THETA = 500000.0
Q_BLOCK = 128

B_WIDTH = D_MODEL // 2
B_HEADS = 8
B_HEAD_DIM = B_WIDTH // B_HEADS
CONV_WIDTH = 4
LRU_C = 8.0

IN_WIDTH = 3 * A_WIDTH + 2 * B_WIDTH

POOL_WINDOWS = (2, 4, 8, 16)
POOL_GROUPS = len(POOL_WINDOWS)
POOL_GROUP_DIM = D_MODEL // POOL_GROUPS

FFN_DIM = 2816
N_EXPERTS = 8
TOP_K = 2
EXPERT_DIM = 3584

NORM_EPS = 1e-6
SUBLN_EPS = 1e-5


def rms_norm(x, g, eps=NORM_EPS):
    xf = x.astype(jnp.float32)
    y = xf * lax.rsqrt(jnp.mean(xf * xf, axis=-1, keepdims=True) + eps)
    return (y * g.astype(jnp.float32)).astype(x.dtype)

def rope_tables(seq):
    inv = ROPE_THETA ** (-jnp.arange(0, ROPE_DIM, 2, dtype=jnp.float32) / ROPE_DIM)
    ang = jnp.arange(seq, dtype=jnp.float32)[:, None] * inv[None, :]
    return jnp.cos(ang), jnp.sin(ang)

def apply_partial_rope(x, cos, sin):
    half = ROPE_DIM // 2
    x1 = x[..., :half].astype(jnp.float32)
    x2 = x[..., half:ROPE_DIM].astype(jnp.float32)
    c = cos[None, :, None, None, :]
    s = sin[None, :, None, None, :]
    rot = jnp.concatenate([x1 * c - x2 * s, x2 * c + x1 * s], axis=-1).astype(x.dtype)
    return jnp.concatenate([rot, x[..., ROPE_DIM:]], axis=-1)

def diff_attention(q, k, v, lam, lam_init, subln_g):
    bsz, seq = q.shape[0], q.shape[1]
    nb = seq // Q_BLOCK
    q = q * (A_QK_DIM ** -0.5)
    qb = q.reshape(bsz, nb, Q_BLOCK, A_HEADS, 2, A_QK_DIM).transpose(1, 0, 2, 3, 4, 5)
    key_pos = jnp.arange(seq)

    def block(args):
        q_blk, bi = args
        s = jnp.einsum("bqhmd,bkhmd->bhmqk", q_blk, k).astype(jnp.float32)
        q_pos = bi * Q_BLOCK + jnp.arange(Q_BLOCK)
        mask = key_pos[None, :] <= q_pos[:, None]
        p = jax.nn.softmax(jnp.where(mask, s, -jnp.inf), axis=-1)
        w = p[:, :, 0] - lam * p[:, :, 1]
        return jnp.einsum("bhqk,bkhd->bqhd", w.astype(v.dtype), v)

    o = lax.map(block, (qb, jnp.arange(nb)))
    o = o.transpose(1, 0, 2, 3, 4).reshape(bsz, seq, A_HEADS, A_V_DIM)
    o = rms_norm(o, subln_g, SUBLN_EPS) * (1.0 - lam_init)
    return o.reshape(bsz, seq, A_WIDTH)

def causal_depthwise_conv(x, w, b):
    y = lax.conv_general_dilated(
        x, w[:, None, :], window_strides=(1,), padding=[(CONV_WIDTH - 1, 0)],
        dimension_numbers=("NWC", "WIO", "NWC"), feature_group_count=x.shape[-1])
    return y + b

def rg_lru(x, wa, ba, wx, bx, lam):
    bsz, seq, ch = x.shape
    xh = x.reshape(bsz, seq, B_HEADS, B_HEAD_DIM)
    r = jax.nn.sigmoid((jnp.einsum("bshi,hij->bshj", xh, wa) + ba).astype(jnp.float32)).reshape(bsz, seq, ch)
    i = jax.nn.sigmoid((jnp.einsum("bshi,hij->bshj", xh, wx) + bx).astype(jnp.float32)).reshape(bsz, seq, ch)
    log_a = -LRU_C * r * jax.nn.softplus(-lam.astype(jnp.float32))
    a = jnp.exp(log_a)
    u = jnp.sqrt(-jnp.expm1(2.0 * log_a)) * (i * x.astype(jnp.float32))

    def combine(left, right):
        a1, b1 = left
        a2, b2 = right
        return a1 * a2, a2 * b1 + b2

    _, h = lax.associative_scan(combine, (a, u), axis=1)
    return h.astype(x.dtype)

def even_mixer(h, w_in, lq1, lk1, lq2, lk2, subln_g, conv_w, conv_b,
               wa, ba, wx, bx, lam_p, w_out, lam_init, cos, sin):
    bsz, seq, _ = h.shape
    proj = h @ w_in
    q, k, v, xb, gb = jnp.split(
        proj, [A_WIDTH, 2 * A_WIDTH, 3 * A_WIDTH, 3 * A_WIDTH + B_WIDTH], axis=-1)
    q = apply_partial_rope(q.reshape(bsz, seq, A_HEADS, 2, A_QK_DIM), cos, sin)
    k = apply_partial_rope(k.reshape(bsz, seq, A_HEADS, 2, A_QK_DIM), cos, sin)
    v = v.reshape(bsz, seq, A_HEADS, A_V_DIM)
    lam = (jnp.exp(jnp.sum(lq1.astype(jnp.float32) * lk1.astype(jnp.float32)))
           - jnp.exp(jnp.sum(lq2.astype(jnp.float32) * lk2.astype(jnp.float32)))
           + lam_init)
    attn = diff_attention(q, k, v, lam, lam_init, subln_g)
    rec = rg_lru(causal_depthwise_conv(xb, conv_w, conv_b), wa, ba, wx, bx, lam_p)
    rec = rec * jax.nn.gelu(gb)
    return jnp.concatenate([attn, rec], axis=-1) @ w_out

def pool_mixer(h, pool_w, pool_scale):
    bsz, seq, _ = h.shape
    hg = h.reshape(bsz, seq, POOL_GROUPS, POOL_GROUP_DIM)
    pos = jnp.arange(seq)
    outs = []
    for g, w in enumerate(POOL_WINDOWS):
        xg = hg[:, :, g].astype(jnp.float32)
        cs = jnp.cumsum(xg, axis=1)
        lower = jnp.pad(cs, ((0, 0), (w, 0), (0, 0)))[:, :seq]
        count = jnp.minimum(pos + 1, w).astype(jnp.float32)[None, :, None]
        outs.append((cs - lower) / count - xg)
    d = jnp.stack(outs, axis=2).astype(h.dtype)
    y = jnp.einsum("bsgc,gcd->bsgd", d, pool_w).reshape(bsz, seq, D_MODEL)
    return y * pool_scale

def swiglu(h, wg, wu, wd):
    return (jax.nn.silu(h @ wg) * (h @ wu)) @ wd

def moe_swiglu(h, router_w, wg, wu, wd):
    bsz, seq, dm = h.shape
    t = h.reshape(-1, dm)
    logits = (t @ router_w).astype(jnp.float32)
    top_val, top_idx = lax.top_k(logits, TOP_K)
    gates = jax.nn.softmax(top_val, axis=-1)
    combine = jnp.sum(jax.nn.one_hot(top_idx, N_EXPERTS, dtype=jnp.float32) * gates[..., None], axis=1)
    out = jnp.zeros_like(t)
    for e in range(N_EXPERTS):
        he = jax.nn.silu(t @ wg[e]) * (t @ wu[e])
        out = out + (combine[:, e:e + 1].astype(t.dtype) * he) @ wd[e]
    return out.reshape(bsz, seq, dm)

def first_inputs(seed: int = 0) -> dict:
    key = jax.random.key(seed)
    ks = iter(jax.random.split(key, 40))
    f32 = jnp.float32

    def nrm(shape, scale):
        return jax.random.normal(next(ks), shape, f32) * scale

    def gain(shape):
        return 1.0 + 0.02 * jax.random.normal(next(ks), shape, f32)

    x = jax.random.normal(next(ks), (BATCH, SEQ, D_MODEL), f32)
    u = jax.random.uniform(next(ks), (N_EVEN, B_WIDTH), f32, 0.9, 0.999)
    s = u ** (1.0 / LRU_C)
    rg_lam = jnp.log(s / (1.0 - s))
    return {
        "x": x,
        "ln_mix_even": gain((N_EVEN, D_MODEL)),
        "w_in_even": nrm((N_EVEN, D_MODEL, IN_WIDTH), D_MODEL ** -0.5),
        "lam_q1": nrm((N_EVEN, A_QK_DIM), 0.1),
        "lam_k1": nrm((N_EVEN, A_QK_DIM), 0.1),
        "lam_q2": nrm((N_EVEN, A_QK_DIM), 0.1),
        "lam_k2": nrm((N_EVEN, A_QK_DIM), 0.1),
        "subln_g": gain((N_EVEN, A_V_DIM)),
        "conv_w": nrm((N_EVEN, CONV_WIDTH, B_WIDTH), CONV_WIDTH ** -0.5),
        "conv_b": nrm((N_EVEN, B_WIDTH), 0.01),
        "rg_wa": nrm((N_EVEN, B_HEADS, B_HEAD_DIM, B_HEAD_DIM), B_HEAD_DIM ** -0.5),
        "rg_ba": nrm((N_EVEN, B_HEADS, B_HEAD_DIM), 0.01),
        "rg_wx": nrm((N_EVEN, B_HEADS, B_HEAD_DIM, B_HEAD_DIM), B_HEAD_DIM ** -0.5),
        "rg_bx": nrm((N_EVEN, B_HEADS, B_HEAD_DIM), 0.01),
        "rg_lam": rg_lam,
        "w_out_even": nrm((N_EVEN, A_WIDTH + B_WIDTH, D_MODEL), (A_WIDTH + B_WIDTH) ** -0.5),
        "ln_ffn_even": gain((N_EVEN, D_MODEL)),
        "ffn_wg": nrm((N_EVEN, D_MODEL, FFN_DIM), D_MODEL ** -0.5),
        "ffn_wu": nrm((N_EVEN, D_MODEL, FFN_DIM), D_MODEL ** -0.5),
        "ffn_wd": nrm((N_EVEN, FFN_DIM, D_MODEL), FFN_DIM ** -0.5),
        "ln_mix_odd": gain((N_ODD, D_MODEL)),
        "pool_w": nrm((N_ODD, POOL_GROUPS, POOL_GROUP_DIM, POOL_GROUP_DIM), POOL_GROUP_DIM ** -0.5),
        "pool_scale": gain((N_ODD, D_MODEL)),
        "ln_ffn_odd": gain((N_ODD, D_MODEL)),
        "router_w": nrm((N_ODD, D_MODEL, N_EXPERTS), D_MODEL ** -0.5),
        "moe_wg": nrm((N_ODD, N_EXPERTS, D_MODEL, EXPERT_DIM), D_MODEL ** -0.5),
        "moe_wu": nrm((N_ODD, N_EXPERTS, D_MODEL, EXPERT_DIM), D_MODEL ** -0.5),
        "moe_wd": nrm((N_ODD, N_EXPERTS, EXPERT_DIM, D_MODEL), EXPERT_DIM ** -0.5),
        "final_g": gain((D_MODEL,)),
    }

def first_block(x, ln_mix_even, w_in_even, lam_q1, lam_k1, lam_q2, lam_k2, subln_g,
              conv_w, conv_b, rg_wa, rg_ba, rg_wx, rg_bx, rg_lam, w_out_even,
              ln_ffn_even, ffn_wg, ffn_wu, ffn_wd, ln_mix_odd, pool_w, pool_scale,
              ln_ffn_odd, router_w, moe_wg, moe_wu, moe_wd, final_g):
    cos, sin = rope_tables(x.shape[1])
    h = x
    for layer in range(DEPTH):
        j = layer // 2
        if layer % 2 == 0:
            lam_init = 0.8 - 0.6 * math.exp(-0.3 * layer)
            h = h + even_mixer(rms_norm(h, ln_mix_even[j]), w_in_even[j],
                               lam_q1[j], lam_k1[j], lam_q2[j], lam_k2[j], subln_g[j],
                               conv_w[j], conv_b[j], rg_wa[j], rg_ba[j], rg_wx[j], rg_bx[j],
                               rg_lam[j], w_out_even[j], lam_init, cos, sin)
            h = h + swiglu(rms_norm(h, ln_ffn_even[j]), ffn_wg[j], ffn_wu[j], ffn_wd[j])
        else:
            h = h + pool_mixer(rms_norm(h, ln_mix_odd[j]), pool_w[j], pool_scale[j])
            h = h + moe_swiglu(rms_norm(h, ln_ffn_odd[j]), router_w[j],
                               moe_wg[j], moe_wu[j], moe_wd[j])
    return rms_norm(h, final_g)


DEPTH_2 = 1

GRID_W = 64
CTX_LEN = 256
CHUNK = 64
F_TINY = 1e-30

DN_HEADS = 4
DN_DK = 128
DN_DV = 128
DN_QK = DN_HEADS * DN_DK
DN_V = DN_HEADS * DN_DV
CONV_K = 3

HG_HEADS = 4
HG_DK = 128
HG_DV = 128
HG_K = HG_HEADS * HG_DK
HG_V = HG_HEADS * HG_DV

N_GROUPS = 4
EXPERTS_PER_GROUP = 8
N_EXPERTS_2 = N_GROUPS * EXPERTS_PER_GROUP
TOP_K_IN_GROUP = 2
D_EXPERT = D_MODEL // 2
MOE_BLOCK = 128

IN_SIZES = (2 * DN_QK + DN_V, DN_V, 2 * DN_HEADS, 2 * DN_HEADS, HG_K, 2 * HG_K, HG_V, HG_V, 2 * D_MODEL)
IN_SPLITS = tuple(sum(IN_SIZES[:i + 1]) for i in range(len(IN_SIZES) - 1))
N_IN = sum(IN_SIZES)


F32 = jnp.float32

def _rmsnorm(x, g):
    xf = x.astype(F32)
    y = xf * lax.rsqrt(jnp.mean(xf * xf, axis=-1, keepdims=True) + NORM_EPS)
    return (y * g.astype(F32)).astype(x.dtype)

def _l2norm(x):
    xf = x.astype(F32)
    return xf * lax.rsqrt(jnp.sum(xf * xf, axis=-1, keepdims=True) + NORM_EPS)

def _masked_exp(diff, mask):
    return jnp.where(mask, jnp.exp(jnp.where(mask, diff, 0.0)), 0.0)

def _gated_rmsnorm(o, z, g):
    bsz, n, h, dv = o.shape
    y = o * lax.rsqrt(jnp.mean(o * o, axis=-1, keepdims=True) + NORM_EPS) * g.astype(F32)
    y = y * jax.nn.silu(z.astype(F32).reshape(bsz, n, h, dv))
    return y.reshape(bsz, n, h * dv).astype(z.dtype)

def _short_conv(x, w):
    pad = CONV_K // 2
    return lax.conv_general_dilated(x, w[:, None, :].astype(x.dtype), window_strides=(1,),
                                    padding=[(pad, pad)], dimension_numbers=('NWC', 'WIO', 'NWC'),
                                    feature_group_count=x.shape[-1])

def _to_col_major(t):
    bsz, n, f = t.shape
    rows = n // GRID_W
    return t.reshape(bsz, rows, GRID_W, f).transpose(0, 2, 1, 3).reshape(bsz, n, f)

def _from_col_major(t):
    bsz, n, f = t.shape
    rows = n // GRID_W
    return t.reshape(bsz, GRID_W, rows, f).transpose(0, 2, 1, 3).reshape(bsz, n, f)

def _rev(t, direction):
    return jnp.flip(t, axis=1) if direction == 1 else t

def _to_chunks(t):
    bsz, n, h = t.shape[:3]
    t = t.reshape(bsz, n // CHUNK, CHUNK, h, *t.shape[3:])
    return jnp.moveaxis(t, (1, 3), (0, 2))

def _from_chunks(t):
    t = jnp.moveaxis(t, (0, 2), (1, 3))
    return t.reshape(t.shape[0], t.shape[1] * t.shape[2], *t.shape[3:])

def gated_delta_chunked(q, k, v, g, beta, s0, return_out):
    q, k, v, g, beta = (_to_chunks(t.astype(F32)) for t in (q, k, v, g, beta))
    dv = v.shape[-1]
    incl = jnp.tril(jnp.ones((CHUNK, CHUNK), bool))
    strict = jnp.tril(jnp.ones((CHUNK, CHUNK), bool), -1)
    gcum = jnp.cumsum(g, axis=-1)
    decay = _masked_exp(gcum[..., :, None] - gcum[..., None, :], incl)
    kb = k * beta[..., None]
    a = jnp.where(strict, jnp.einsum('nbhik,nbhjk->nbhij', kb, k) * decay, 0.0)
    rhs = jnp.concatenate([v * beta[..., None], kb * jnp.exp(gcum)[..., None]], axis=-1)
    sol = lax.linalg.triangular_solve(a, rhs, left_side=True, lower=True, unit_diagonal=True)
    u, w = sol[..., :dv], sol[..., dv:]

    def step(s, inp):
        qc, kc, uc, wc, gc, dc = inp
        v_new = uc - jnp.einsum('bhck,bhkv->bhcv', wc, s)
        g_last = gc[..., -1]
        s_new = s * jnp.exp(g_last)[..., None, None] + jnp.einsum(
            'bhck,bhcv->bhkv', kc * jnp.exp(g_last[..., None] - gc)[..., None], v_new)
        if not return_out:
            return s_new, None
        o = jnp.einsum('bhck,bhkv->bhcv', qc * jnp.exp(gc)[..., None], s) + jnp.einsum(
            'bhij,bhjv->bhiv', jnp.einsum('bhik,bhjk->bhij', qc, kc) * dc, v_new)
        return s_new, o

    s_fin, o = lax.scan(step, s0.astype(F32), (q, k, u, w, gcum, decay))
    return (_from_chunks(o) if return_out else None), s_fin

def gla_chunked(q, k, v, log_f, s0, return_out):
    q, k, v, log_f = (_to_chunks(t.astype(F32)) for t in (q, k, v, log_f))
    gcum = jnp.cumsum(log_f, axis=3)
    incl = jnp.tril(jnp.ones((CHUNK, CHUNK), bool))[..., None]

    def step(s, inp):
        qc, kc, vc, gc = inp
        g_last = gc[:, :, -1]
        s_new = s * jnp.exp(g_last)[..., None] + jnp.einsum(
            'bhck,bhcv->bhkv', kc * jnp.exp(g_last[:, :, None] - gc), vc)
        if not return_out:
            return s_new, None
        rel = _masked_exp(gc[:, :, :, None] - gc[:, :, None], incl)
        att = jnp.einsum('bhik,bhjk,bhijk->bhij', qc, kc, rel)
        o = jnp.einsum('bhck,bhkv->bhcv', qc * jnp.exp(gc), s) + jnp.einsum('bhij,bhjv->bhiv', att, vc)
        return s_new, o

    s_fin, o = lax.scan(step, s0.astype(F32), (q, k, v, gcum))
    return (_from_chunks(o) if return_out else None), s_fin

def _dn_inputs(qkv, b, a, conv_w, a_log, dt_bias):
    bsz, n = qkv.shape[:2]
    qkv = jax.nn.silu(_short_conv(qkv, conv_w))
    q, k, v = jnp.split(qkv, [DN_QK, 2 * DN_QK], axis=-1)
    q = _l2norm(q.reshape(bsz, n, DN_HEADS, DN_DK)) * (DN_DK ** -0.5)
    k = _l2norm(k.reshape(bsz, n, DN_HEADS, DN_DK))
    v = v.reshape(bsz, n, DN_HEADS, DN_DV)
    beta = jax.nn.sigmoid(b.astype(F32).reshape(bsz, n, 2, DN_HEADS))
    g = -jnp.exp(a_log.astype(F32)) * jax.nn.softplus(
        a.astype(F32).reshape(bsz, n, 2, DN_HEADS) + dt_bias.astype(F32))
    return q, k, v, beta, g

def _deltanet_scans(lat, ctx, ctx_out):
    xq, xk, xv, xb, xg = lat
    cq, ck, cv, cb, cg = ctx
    o_x, o_c = 0.0, 0.0
    for d in range(2):
        s0 = jnp.zeros((xq.shape[0], DN_HEADS, DN_DK, DN_DV), F32)
        oc, s_ctx = gated_delta_chunked(*(_rev(t, d) for t in (cq, ck, cv, cg[:, :, d], cb[:, :, d])), s0, ctx_out)
        ox, _ = gated_delta_chunked(*(_rev(t, d) for t in (xq, xk, xv, xg[:, :, d], xb[:, :, d])), s_ctx, True)
        o_x = o_x + _rev(ox, d)
        if ctx_out:
            o_c = o_c + _rev(oc, d)
    return o_x, (o_c if ctx_out else None)

def _hg_inputs(q, f2, i, lb):
    bsz, n = q.shape[:2]
    q = jax.nn.silu(q.astype(F32)).reshape(bsz, n, HG_HEADS, HG_DK)
    z = f2.astype(F32).reshape(bsz, n, 2, HG_HEADS, HG_DK)
    f = lb + (1.0 - lb) * jax.nn.sigmoid(z)
    log_f = jnp.log(jnp.maximum(f, F_TINY))
    k = (1.0 - lb) * jax.nn.sigmoid(-z)
    v = i.astype(F32).reshape(bsz, n, HG_HEADS, HG_DV)
    return q, k, log_f, v

def _hgrn2_scans(lat, ctx, ctx_out):
    xq, xk, xlf, xv = lat
    cq, ck, clf, cv = ctx
    o_x, o_c = 0.0, 0.0
    for d in range(2):
        s0 = jnp.zeros((xq.shape[0], HG_HEADS, HG_DK, HG_DV), F32)
        oc, s_ctx = gla_chunked(*(_rev(t, d) for t in (cq, ck[:, :, d], cv, clf[:, :, d])), s0, ctx_out)
        ox, _ = gla_chunked(*(_rev(t, d) for t in (xq, xk[:, :, d], xv, xlf[:, :, d])), s_ctx, True)
        o_x = o_x + _rev(ox, d)
        if ctx_out:
            o_c = o_c + _rev(oc, d)
    return o_x, (o_c if ctx_out else None)

def hybrid_mixer(hx, hc, w_in, dn_conv, dn_a_log, dn_dt_bias, dn_norm_g, lb, hg_norm_g,
                 w_br_dn, w_br_hg, w_out, ctx_out):
    bsz, n_lat = hx.shape[:2]
    n_ctx = hc.shape[1]
    proj = jnp.concatenate([hc, hx], axis=1) @ w_in
    pc = jnp.split(proj[:, :n_ctx], IN_SPLITS, axis=-1)
    px = jnp.split(proj[:, n_ctx:], IN_SPLITS, axis=-1)
    odn_x, odn_c = _deltanet_scans(_dn_inputs(px[0], px[2], px[3], dn_conv, dn_a_log, dn_dt_bias),
                                   _dn_inputs(pc[0], pc[2], pc[3], dn_conv, dn_a_log, dn_dt_bias), ctx_out)
    ohg_x, ohg_c = _hgrn2_scans(_hg_inputs(*(_to_col_major(t) for t in (px[4], px[5], px[6])), lb),
                                _hg_inputs(pc[4], pc[5], pc[6], lb), ctx_out)
    ohg_x = _from_col_major(ohg_x.reshape(bsz, n_lat, HG_V)).reshape(bsz, n_lat, HG_HEADS, HG_DV)

    def merge(parts, odn, ohg):
        br_dn = _gated_rmsnorm(odn, parts[1], dn_norm_g) @ w_br_dn
        br_hg = _gated_rmsnorm(ohg, parts[7], hg_norm_g) @ w_br_hg
        gate_dn, gate_hg = jnp.split(parts[8], 2, axis=-1)
        return (jax.nn.sigmoid(gate_dn) * br_dn + jax.nn.sigmoid(gate_hg) * br_hg) @ w_out

    y_x = merge(px, odn_x, ohg_x)
    y_c = merge(pc, odn_c, ohg_c) if ctx_out else None
    return y_x, y_c

def hier_moe(h, w_rg, b_rg, w_re, b_re, w_gate, w_up, w_down):
    n_tok, d = h.shape
    grp_logits = (h @ w_rg + b_rg).astype(F32)
    grp_sel = jnp.argmax(grp_logits, axis=-1)
    grp_p = jnp.take_along_axis(jax.nn.softmax(grp_logits, axis=-1), grp_sel[:, None], axis=-1)
    exp_logits = (h @ w_re + b_re).astype(F32).reshape(n_tok, N_GROUPS, EXPERTS_PER_GROUP)
    in_logits = jnp.take_along_axis(exp_logits, grp_sel[:, None, None], axis=1)[:, 0]
    top_p, top_j = lax.top_k(jax.nn.softmax(in_logits, axis=-1), TOP_K_IN_GROUP)
    gate = grp_p * top_p / jnp.sum(top_p, axis=-1, keepdims=True)
    expert = grp_sel[:, None] * EXPERTS_PER_GROUP + top_j
    n_asg = n_tok * TOP_K_IN_GROUP
    e_flat = expert.reshape(n_asg)
    order = jnp.argsort(e_flat)
    e_sorted = e_flat[order]
    tok_sorted = order // TOP_K_IN_GROUP
    gate_sorted = gate.reshape(n_asg)[order]
    counts = jnp.bincount(e_flat, length=N_EXPERTS_2)
    padded = (counts + MOE_BLOCK - 1) // MOE_BLOCK * MOE_BLOCK
    pad_end = jnp.cumsum(padded)
    pad_start = pad_end - padded
    start = jnp.cumsum(counts) - counts
    dest = pad_start[e_sorted] + jnp.arange(n_asg) - start[e_sorted]
    n_blocks = (n_asg + N_EXPERTS_2 * (MOE_BLOCK - 1) + MOE_BLOCK - 1) // MOE_BLOCK
    rows = jnp.zeros((n_blocks * MOE_BLOCK, d), h.dtype).at[dest].set(h[tok_sorted])
    block_expert = jnp.minimum(jnp.searchsorted(pad_end, jnp.arange(n_blocks) * MOE_BLOCK, side='right'),
                               N_EXPERTS_2 - 1)

    def expert_block(args):
        xb, e = args
        return (jax.nn.silu(xb @ w_gate[e]) * (xb @ w_up[e])) @ w_down[e]

    out = lax.map(expert_block, (rows.reshape(n_blocks, MOE_BLOCK, d), block_expert)).reshape(-1, d)
    contrib = (out[dest] * gate_sorted[:, None]).astype(h.dtype)
    return jnp.zeros((n_tok, d), h.dtype).at[tok_sorted].add(contrib)

def second_inputs(seed: int = 0) -> dict:
    key = jax.random.key(seed)
    ks = iter(jax.random.split(key, 26))
    D, L = D_MODEL, DEPTH_2

    def nrm(shape, scale):
        return jax.random.normal(next(ks), shape, F32) * scale

    x = nrm((BATCH, SEQ, D), 1.0)
    c = nrm((BATCH, D), 1.0)
    ctx = nrm((BATCH, CTX_LEN, D), 1.0)
    c_ctx = nrm((D,), 1.0)
    w_ada = nrm((L, D, 6 * D), 0.5 * D ** -0.5)
    b_ada = nrm((L, 6 * D), 0.02)
    g_mix = 1.0 + nrm((L, D), 0.02)
    g_ffn = 1.0 + nrm((L, D), 0.02)
    g_final = 1.0 + nrm((D,), 0.02)
    w_in = nrm((L, D, N_IN), D ** -0.5)
    dn_conv = nrm((L, CONV_K, 2 * DN_QK + DN_V), CONV_K ** -0.5)
    dn_a_log = jnp.log(jax.random.uniform(next(ks), (L, 2, DN_HEADS), F32, 1.0, 16.0))
    dt = jnp.exp(jax.random.uniform(next(ks), (L, 2, DN_HEADS), F32, math.log(1e-3), math.log(1e-1)))
    dn_dt_bias = dt + jnp.log(-jnp.expm1(-dt))
    dn_norm_g = 1.0 + nrm((L, DN_DV), 0.02)
    hg_lb_logits = nrm((L, HG_K), 0.5)
    hg_norm_g = 1.0 + nrm((L, HG_DV), 0.02)
    w_br_dn = nrm((L, DN_V, D), DN_V ** -0.5)
    w_br_hg = nrm((L, HG_V, D), HG_V ** -0.5)
    w_out = nrm((L, D, D), D ** -0.5)
    w_router_grp = nrm((L, D, N_GROUPS), D ** -0.5)
    b_router_grp = nrm((L, N_GROUPS), 0.01)
    w_router_exp = nrm((L, D, N_EXPERTS_2), D ** -0.5)
    b_router_exp = nrm((L, N_EXPERTS_2), 0.01)
    w_exp_gate = nrm((L, N_EXPERTS_2, D, D_EXPERT), D ** -0.5)
    w_exp_up = nrm((L, N_EXPERTS_2, D, D_EXPERT), D ** -0.5)
    w_exp_down = nrm((L, N_EXPERTS_2, D_EXPERT, D), D_EXPERT ** -0.5)
    return {'x': x, 'c': c, 'ctx': ctx, 'c_ctx': c_ctx, 'w_ada': w_ada, 'b_ada': b_ada,
            'g_mix': g_mix, 'g_ffn': g_ffn, 'g_final': g_final, 'w_in': w_in, 'dn_conv': dn_conv,
            'dn_a_log': dn_a_log, 'dn_dt_bias': dn_dt_bias, 'dn_norm_g': dn_norm_g,
            'hg_lb_logits': hg_lb_logits, 'hg_norm_g': hg_norm_g, 'w_br_dn': w_br_dn,
            'w_br_hg': w_br_hg, 'w_out': w_out, 'w_router_grp': w_router_grp,
            'b_router_grp': b_router_grp, 'w_router_exp': w_router_exp, 'b_router_exp': b_router_exp,
            'w_exp_gate': w_exp_gate, 'w_exp_up': w_exp_up, 'w_exp_down': w_exp_down}

def second_block(x, c, ctx, c_ctx, w_ada, b_ada, g_mix, g_ffn, g_final, w_in, dn_conv, dn_a_log,
              dn_dt_bias, dn_norm_g, hg_lb_logits, hg_norm_g, w_br_dn, w_br_hg, w_out,
              w_router_grp, b_router_grp, w_router_exp, b_router_exp, w_exp_gate, w_exp_up,
              w_exp_down):
    bsz, n_lat, d = x.shape
    n_ctx = ctx.shape[1]
    lb_w = jax.nn.softmax(hg_lb_logits.astype(F32), axis=0)
    lower_bounds = jnp.cumsum(lb_w, axis=0) - lb_w[0]
    s_c = jax.nn.silu(c)
    s_cc = jax.nn.silu(c_ctx)
    h_ctx = ctx
    for layer in range(DEPTH_2):
        last = layer == DEPTH_2 - 1
        mod_x = jnp.split((s_c @ w_ada[layer] + b_ada[layer])[:, None, :], 6, axis=-1)
        mod_c = jnp.split(s_cc @ w_ada[layer] + b_ada[layer], 6, axis=-1)
        hx = _rmsnorm(x, g_mix[layer]) * (1.0 + mod_x[1]) + mod_x[0]
        hc = _rmsnorm(h_ctx, g_mix[layer]) * (1.0 + mod_c[1]) + mod_c[0]
        y_x, y_c = hybrid_mixer(hx, hc, w_in[layer], dn_conv[layer], dn_a_log[layer], dn_dt_bias[layer],
                                dn_norm_g[layer], lower_bounds[layer].reshape(HG_HEADS, HG_DK),
                                hg_norm_g[layer], w_br_dn[layer], w_br_hg[layer], w_out[layer],
                                not last)
        x = x + mod_x[2] * y_x
        hx = (_rmsnorm(x, g_ffn[layer]) * (1.0 + mod_x[4]) + mod_x[3]).reshape(-1, d)
        moe_args = (w_router_grp[layer], b_router_grp[layer], w_router_exp[layer], b_router_exp[layer],
                    w_exp_gate[layer], w_exp_up[layer], w_exp_down[layer])
        if last:
            f_x = hier_moe(hx, *moe_args)
        else:
            h_ctx = h_ctx + mod_c[2] * y_c
            hc = (_rmsnorm(h_ctx, g_ffn[layer]) * (1.0 + mod_c[4]) + mod_c[3]).reshape(-1, d)
            f_all = hier_moe(jnp.concatenate([hc, hx], axis=0), *moe_args)
            h_ctx = h_ctx + mod_c[5] * f_all[:bsz * n_ctx].reshape(bsz, n_ctx, d)
            f_x = f_all[bsz * n_ctx:]
        x = x + mod_x[5] * f_x.reshape(bsz, n_lat, d)
    return _rmsnorm(x, g_final)


def setup_inputs(seed=0):
    out = dict(first_inputs(seed))
    for name, value in second_inputs(seed + 1).items():
        if name != "x":
            out[name + "_2"] = value
    return out


def reference(
    x, ln_mix_even, w_in_even, lam_q1, lam_k1, lam_q2, lam_k2, subln_g, conv_w, conv_b, rg_wa,
    rg_ba, rg_wx, rg_bx, rg_lam, w_out_even, ln_ffn_even, ffn_wg, ffn_wu, ffn_wd, ln_mix_odd,
    pool_w, pool_scale, ln_ffn_odd, router_w, moe_wg, moe_wu, moe_wd, final_g, c_2, ctx_2,
    c_ctx_2, w_ada_2, b_ada_2, g_mix_2, g_ffn_2, g_final_2, w_in_2, dn_conv_2, dn_a_log_2,
    dn_dt_bias_2, dn_norm_g_2, hg_lb_logits_2, hg_norm_g_2, w_br_dn_2, w_br_hg_2, w_out_2,
    w_router_grp_2, b_router_grp_2, w_router_exp_2, b_router_exp_2, w_exp_gate_2, w_exp_up_2,
    w_exp_down_2,
):
    x = first_block(
        x, ln_mix_even, w_in_even, lam_q1, lam_k1, lam_q2, lam_k2, subln_g, conv_w, conv_b,
        rg_wa, rg_ba, rg_wx, rg_bx, rg_lam, w_out_even, ln_ffn_even, ffn_wg, ffn_wu, ffn_wd,
        ln_mix_odd, pool_w, pool_scale, ln_ffn_odd, router_w, moe_wg, moe_wu, moe_wd, final_g,
    )
    return second_block(
        x, c_2, ctx_2, c_ctx_2, w_ada_2, b_ada_2, g_mix_2, g_ffn_2, g_final_2, w_in_2,
        dn_conv_2, dn_a_log_2, dn_dt_bias_2, dn_norm_g_2, hg_lb_logits_2, hg_norm_g_2,
        w_br_dn_2, w_br_hg_2, w_out_2, w_router_grp_2, b_router_grp_2, w_router_exp_2,
        b_router_exp_2, w_exp_gate_2, w_exp_up_2, w_exp_down_2,
    )


_drawn_inputs = setup_inputs


def setup_inputs(seed=0):
    import zlib

    import numpy as np

    out = dict(_drawn_inputs(seed))
    spreads = {}
    factors = {'rg_ba': 8.0,
     'rg_bx': 8.0,
     'ctx_2': 4.888,
     'c_ctx_2': 8.0,
     'b_ada_2': 3.017,
     'g_mix_2': 8.0,
     'g_ffn_2': 5.401,
     'g_final_2': 7.408,
     'dn_norm_g_2': 8.0,
     'hg_norm_g_2': 8.0,
     'b_router_grp_2': 8.0,
     'b_router_exp_2': 35.772}
    for name, (base, spread) in spreads.items():
        noise = np.random.default_rng([zlib.crc32(name.encode()), seed]).standard_normal(out[name].shape)
        drawn = base * np.exp(spread * noise) if base else spread * noise
        out[name] = jnp.asarray(drawn.astype(out[name].dtype))
    for name, factor in factors.items():
        out[name] = (out[name] * factor).astype(out[name].dtype)
    return out
```

```python
import math
from contextlib import ExitStack

import numpy as np

import concourse.bass as bass
from concourse import mybir

F32 = mybir.dt.float32
ALU = mybir.AluOpType
ACT = mybir.ActivationFunctionType
AX = mybir.AxisListType

P = 128
D = 1024
KC = D // P
S = 256
NT = S // P
H = 4
EPS = 1e-6
SUB_EPS = 1e-5
FFN = 2816
E1, F1 = 8, 3584
E2, F2 = 32, 512
UW = 512
C1, C2 = 96, 64
NSLOT = 6
SLOT = 4096
LEVELS = (1, 2, 4, 8, 16, 32, 64)
BIG = 1.0e30
LN_TINY = 1e-30

C_ID, C_ONE, C_LE, C_GE, C_IOTA = 0, 128, 256, 384, 512
C_LVL = 640
N_CONST = C_LVL + 14 * 128
C1_ROT, C1_COS, C1_SIN, C1_MASK = 0, 128, 384, 640
N_CONST1 = 896

ROWS_A = [("ln_mix_even", 8), ("subln_g", 1), ("conv_w", 16), ("conv_b", 4), ("rg_ba", 4), ("rg_bx", 4),
          ("rg_lam", 4), ("ln_ffn_even", 8), ("ln_mix_odd", 8), ("ln_ffn_odd", 8)]
ROWS_B = [("c_2", 8), ("c_ctx_2", 8), ("b_ada_2", 48), ("g_mix_2", 8), ("g_ffn_2", 8), ("dn_conv_2", 36),
          ("dn_norm_g_2", 1), ("hg_lb_logits_2", 4), ("hg_norm_g_2", 1)]


def row_offsets(rows):
    at, out = 0, {}
    for name, n in rows:
        out[name] = (at, n)
        at += n
    return out, at


OFF_A, NA = row_offsets(ROWS_A)
OFF_B, NB = row_offsets(ROWS_B)


SHARED = {
    "pe_mixer1": [("colsT_ready", 1), ("qk_proj", 4), ("v_proj", 1), ("xb_proj", 1), ("gb_proj", 1),
        ("rot_ready", 1), ("scores_ready", 1), ("wT_ready", 1), ("o_ready", 1), ("oT_ready", 1), ("scores_ready", 1),
        ("wT_ready", 1), ("o_ready", 1), ("oT_ready", 1), ("gates_ready", 1), ("y_ready", 2), ("pool_ready", 1),
        ("pool_y", 1), ("logits_ready", 1), ("rank1_sum", 1)],
    "pe_deltanet": [("k_proj", 4), ("v2_proj", 4), ("q_proj", 1), ("ba_proj", 1), ("k_ss", 1), ("gcs_sum", 1),
        ("kT_ready", 1), ("vT_ready", 1), ("q_ss", 1)],
    "pe_hgrn2": [("zd_proj", 1), ("o_ss", 1), ("hq_proj", 1), ("f_proj", 1), ("hi_proj", 1), ("kdT_ready", 1),
        ("Sg_sum", 1), ("attX_sum", 1), ("og_sum", 1), ("f_proj", 1), ("hz_proj", 1), ("gate_proj", 1),
        ("kdT_ready", 1), ("Sg_sum", 1), ("attX_sum", 1), ("og_sum", 1), ("o_ss", 1), ("gate_proj", 3), ("br", 8),
        ("grow_sum", 1), ("y2_ready", 2), ("grow_sum", 1), ("logits_ready", 1), ("rank2_sum", 1)],
    "ve_mixer1": [("eps_ready", 1), ("cols_ready", 1), ("lam_dot", 1), ("nl_ready", 1), ("qk_copied", 4),
        ("v_copied", 1), ("xb_copied", 1), ("xc_ready", 1), ("rope_done", 1), ("s_shifted", 1), ("w_ready", 1),
        ("wT_copied", 1), ("o_copied", 1), ("o_ms", 1), ("o_normed", 1), ("o_copied", 1), ("s_shifted", 1),
        ("w_ready", 1), ("wT_copied", 1), ("o_copied", 1), ("o_ms", 1), ("o_normed", 1), ("o_copied", 1),
        ("mod_ready", 1), ("gelu_in", 1), ("log_a", 1), ("one_minus", 1), ("rec_ready", 1), ("poolT_copied", 1),
        ("hTc_ready", 1), ("sel1_ready", 1), ("top1_diff", 1), ("rounds1_ready", 1)],
    "ve_deltanet": [("kraw", 1), ("kc_conv", 1), ("vraw", 1), ("vc_conv", 1), ("qraw", 1), ("qc_conv", 1),
        ("g_pre", 1), ("gdec_ready", 1), ("gcs_ready", 1), ("bg_ready", 1), ("kF_ready", 1), ("vTok_ready", 1),
        ("qF_ready", 1)],
    "ve_hgrn2": [("y_gated", 1), ("lb_shift", 1), ("kk_ready", 1), ("f_parts", 1), ("gg_ready", 1), ("kd_ready", 1),
        ("hv_ready", 1), ("qe_ready", 1), ("Sg_ready", 1), ("attX_ready", 1), ("og_ready", 1), ("kk_ready", 1),
        ("f_parts", 1), ("gg_ready", 1), ("kd_ready", 1), ("qe_ready", 1), ("Sg_ready", 1), ("attX_ready", 1),
        ("og_ready", 1), ("y_gated", 1), ("dg_ready", 1), ("br_read", 4), ("mg_ready", 1), ("dg_ready", 1),
        ("grp_shift", 1), ("sel2_ready", 1), ("top2_diff", 1), ("rounds2_ready", 1)],
    "ve_end": [("result", 1)],
    "ac_mixer1": [("lam_exp", 1), ("nl_ln", 1), ("c_silu", 1), ("gb_copied", 1), ("s_exp", 1), ("o_rstd", 1),
        ("s_exp", 1), ("o_rstd", 1), ("gelu_tanh", 1), ("rg_sig", 1), ("rg_exp", 1), ("rg_sqrt", 1), ("top1_exp", 1)],
    "ac_deltanet": [("k_sq", 1), ("vc_ready", 1), ("ba_read", 1), ("sp_ln", 1), ("k_rs", 1), ("egc_ready", 1),
        ("kTok_ready", 1), ("q_sq", 1), ("q_rs", 1)],
    "ac_hgrn2": [("o_sq", 1), ("z_silu", 1), ("rs_done", 1), ("lb_exp", 1), ("hq_ready", 1), ("f_sig", 1),
        ("f_ln", 1), ("kd_exp", 1), ("eg_exp", 1), ("kdTok_ready", 1), ("f_sig", 1), ("f_ln", 1), ("kd_exp", 1),
        ("eg_exp", 1), ("z_silu", 1), ("gate_sig", 1), ("kdTok_ready", 1), ("o_sq", 1), ("rs_done", 1),
        ("gate_sig", 3), ("grow_ready", 1), ("frow_ready", 1), ("grp_exp", 1), ("top2_exp", 1)],
}


def constants():
    i = np.arange(P)
    t = np.zeros((P, N_CONST), np.float32)
    t[:, C_ID:C_ID + P] = np.eye(P)
    t[:, C_ONE:C_ONE + P] = 1.0
    t[:, C_LE:C_LE + P] = i[:, None] <= i[None, :]
    t[:, C_GE:C_GE + P] = i[:, None] >= i[None, :]
    t[:, C_IOTA:C_IOTA + P] = i[None, :]
    for n, b in enumerate(LEVELS):
        m = (i[:, None] // (2 * b) == i[None, :] // (2 * b)) & (i[:, None] // b % 2 == 1) & (i[None, :] // b % 2 == 0)
        t[:, C_LVL + 256 * n:C_LVL + 256 * n + P] = m
        t[:, C_LVL + 256 * n + P:C_LVL + 256 * n + 2 * P] = m.T
    t1 = np.zeros((P, N_CONST1), np.float32)
    pos = np.arange(S, dtype=np.float32)
    inv = np.float32(500000.0) ** (-np.arange(0, 16, 2, dtype=np.float32) / np.float32(16))
    ang = (pos[None, :] * inv[:, None]).astype(np.float32)
    t1[:, C1_COS:C1_COS + S] = 1.0
    for m in (0, 64):
        for d in range(8):
            t1[m + d + 8, C1_ROT + m + d] = -1.0
            t1[m + d, C1_ROT + m + d + 8] = 1.0
        for half in (0, 8):
            t1[m + half:m + half + 8, C1_COS:C1_COS + S] = np.cos(ang)
            t1[m + half:m + half + 8, C1_SIN:C1_SIN + S] = np.sin(ang)
    t1[:, C1_MASK + P:C1_MASK + 2 * P] = np.where(i[None, :] <= i[:, None], 0.0, -BIG)
    band = np.zeros((S, 4, S), np.float32)
    s_, t_ = np.arange(S)[:, None], np.arange(S)[None, :]
    for g, w in enumerate((2, 4, 8, 16)):
        inside = (s_ <= t_) & (s_ > t_ - w)
        band[:, g] = inside / np.minimum(t_ + 1, w) - (s_ == t_)
    return {"k_table": t, "k_table1": t1, "k_band": band}


def build(nc, ins, out):
    ctx = ExitStack()
    with ctx:
        sems, count = {}, {}

        def sem(name):
            if name not in sems:
                sems[name] = ctx.enter_context(nc.semaphore(name))
            return sems[name]

        place = {}
        for group, names in SHARED.items():
            seen = 0
            for name, n in names:
                for _ in range(n):
                    seen += 1
                    k = sum(1 for key in place if key[0] == name) + 1
                    place[name, k] = (group, seen)
        shared = {name for name, _ in place}
        emitted = {}

        def inc(name):
            if name not in shared:
                return sem(name)
            k = emitted[name] = emitted.get(name, 0) + 1
            group, value = place[name, k]
            emitted[group] = emitted.get(group, 0) + 1
            assert emitted[group] == value, (name, k)
            return sem(group)

        def at(name, value):
            if name not in shared:
                return sem(name), value
            group, total = place[name, value]
            return sem(group), total

        def sb(name, shape):
            return ctx.enter_context(nc.sbuf_tensor(name, shape, F32))

        ring = sb("ring", [P, NSLOT, SLOT])
        res = sb("res", [P, NT, D])
        hT = sb("hT", [P, KC, 2 * S])
        table = sb("table", [P, N_CONST])
        rowsA = sb("rowsA", [P, P])
        rowsB = sb("rowsB", [P, P])
        pA = sb("pA", [P, NA])
        pB = sb("pB", [P, NB])
        small = sb("small", [P, 640])
        wba = sb("wba", [P, KC, 16])
        NAR = 18700
        arena = sb("arena", [P, NAR])
        ps = ctx.enter_context(nc.psum_tensor("ps", [P, 8, 512], F32))

        def area(off, *dims):
            n = int(np.prod(dims))
            assert off + n <= NAR, (off, dims)
            v = arena[:, off:off + n]
            if len(dims) == 2:
                return v.rearrange("p (a b) -> p a b", a=dims[0])
            if len(dims) == 3:
                return v.rearrange("p (a b c) -> p a b c", a=dims[0], b=dims[1])
            return v

        taken = [0]

        def sm(*dims):
            n = int(np.prod(dims))
            o = taken[0]
            taken[0] += n
            assert taken[0] <= 640
            v = small[:, o:o + n]
            if len(dims) == 2:
                v = v.rearrange("p (a b) -> p a b", a=dims[0])
            if len(dims) == 3:
                v = v.rearrange("p (a b c) -> p a b c", a=dims[0], b=dims[1])
            return v

        def bank(b, *dims):
            v = ps[:, b, :]
            if len(dims) == 2:
                v = ps[:, b, 0:dims[0] * dims[1]].rearrange("p (a b) -> p a b", a=dims[0])
            return v

        ident = table[:, C_ID:C_ID + P]
        ones = table[:, C_ONE:C_ONE + P]
        tri_le = table[:, C_LE:C_LE + P]
        tri_ge = table[:, C_GE:C_GE + P]
        iota = table[:, C_IOTA:C_IOTA + P]

        def level_mask(n, transposed):
            o = C_LVL + 256 * n + (P if transposed else 0)
            return table[:, o:o + P]

        def colA(name, i=0, n=1):
            o = OFF_A[name][0] + i
            return pA[:, o:o + n]

        def colB(name, i=0, n=1):
            o = OFF_B[name][0] + i
            return pB[:, o:o + n]

        def over(ap, n):
            shape = list(ap.shape)
            return ap[..., None].to_broadcast(shape + [n])

        def rep(ap, m):
            return ap[:, None, :].to_broadcast([P, m, ap.shape[-1]])

        xn = area(0, NT, D)
        const1 = area(17500, N_CONST1)
        rot, cosT, sinT, amask = (const1[:, C1_ROT:C1_ROT + P], const1[:, C1_COS:C1_COS + S],
                                  const1[:, C1_SIN:C1_SIN + S], const1[:, C1_MASK:C1_MASK + S])
        qk = area(2048, 8, S)
        vtok = area(4096, NT, 512)
        xpad = area(5120, 4, S + 3)
        gbF = area(6160, 4, S)
        xc = area(7184, 4, S)
        sc = area(8208, 8, S)
        wts = area(10256, 4, S)
        wT = area(11280, 2, 4, P)
        ot = area(12304, 4, P)
        osq = area(12816, 4, P)
        rtmp = area(13328, 2, S)
        gel = area(13840, 4, S)
        gt = area(14864, 4, S)
        rg_r = area(8208, 4, S)
        rg_i = area(9232, 4, S)
        rg_a = area(10256, 4, S)
        rg_u = area(11280, 4, S)
        rg_h = area(15900, 4, S)
        wgate = area(0, 2, 4, P)
        modrow = area(1024, 2, 512)
        mixT = hT[:, :, S:2 * S]
        hTx = hT[:, :, 0:S]
        actb = area(2048, 4, S)
        sgb = area(3072, 4, S)
        brow = area(4096, D)
        poolT = area(5120, KC, S)
        rw1 = area(17000, KC, E1)

        xnA = xn
        m_act = area(12288, 8, P)
        m_sg = area(2048, 8, P)
        xgT = area(3072, 2, KC * P)
        m_G = area(5120, NT, P)
        m_Gc = area(5376, NT, P)
        GcT = area(5632, 2, NT, P)
        ysb = area(6144, D)
        facc = area(7168, NT, D)

        ss, ms, lnv, rstd = sm(NT), sm(NT), sm(NT), sm(NT)
        lamv = area(16924, 4, 64)
        lams = sm(8)
        mx, smx, rsm = sm(8), sm(8), sm(8)
        o4, o4b, o4c = sm(4), sm(4), sm(4)
        nl, nl2, nl3 = sm(4), sm(4), sm(4)
        mx1, mx2, dm, e2_, g1_, g2_ = sm(NT), sm(NT), sm(NT), sm(NT), sm(NT), sm(NT)
        i1_ = sm(NT)
        lgt = area(9216, NT, E2)
        lgm = area(9280, NT, E2)
        oh1 = area(9408, NT, E2)
        oh2 = area(9472, NT, E2)
        seli = area(9536, NT, E2)
        rank = area(9600, NT, E2 + 2)
        comb = area(9700, NT, E2 + 2)
        cmax, rnd, rndt = sm(1), sm(1), sm(1)
        rounds_i = [ctx.enter_context(nc.sbuf_tensor("rounds%d" % i, [P, 1], mybir.dt.int32)) for i in range(2)]

        mod = sm(48, 2)
        scT = sm(KC, 2)
        gA, gC, gM = sm(KC), sm(KC), sm(KC)
        alog, dtb = sm(8), sm(8)
        beta, gdec, gcs, egc, bg = sm(4, 8), sm(4, 8), sm(4, 8), sm(4, 8), sm(4, 8)
        spa = sm(4, 8)
        kdl = [sm(H) for _ in range(2)]
        egl = [sm(H) for _ in range(2)]
        lbl, lbe, lbw, lb, omlb = sm(H), sm(H), sm(H), sm(H), sm(H)
        gsum, gmx, gprob = sm(NT), sm(NT), sm(NT)
        hTc = hT[:, :, S:2 * S]
        cres = facc
        fgrow = area(15360, D)
        kF = area(0, 4, 512)
        kTok = area(2048, 4, H, P)
        vTok = area(4096, 4, H, P)
        qF = area(6144, 4, S)
        oF = area(7168, 4, S)
        xraw = area(8192, 4, 2, S + 2)
        kc = area(10256, 4, 512)
        sq = area(12304, 4, 512)
        vc = area(14352, 4, 512)
        qc = area(16400, 4, S)
        WK = [[area(8192 + 4608 * d + 512 * i, H, P) for i in range(9)] for d in range(2)]
        Sd = [area(17408 + 512 * d, H, P) for d in range(2)]
        zs = area(8192, 4, S)
        rs = area(9216, 4, S)
        hq = area(0, 4, S)
        hv = area(1024, 4, 512)
        og = area(3072, 4, S)
        kk = area(4096, 4, 512)
        hxp = area(16384, KC, S)
        Sg = area(6144, H, P)
        attX = area(6656, H, P)
        ff = area(8192, 4, 512)
        f2 = area(10240, 4, 512)
        gg = area(12288, 4, 512)
        Wd = area(14336, 4, S)
        Wx = area(15360, 4, S)
        qW = area(16384, 4, S)
        kW = area(17408, 4, S)
        attT = area(10240, NT, H, P)
        atmp = area(11264, NT, H, P)
        kdTok = area(15360, NT, H, P)
        qe = area(8192, 4, S)
        eg = area(9216, 4, S)
        zh = hT[:, 0:4, S:2 * S]
        gd0 = hT[:, 4:8, S:2 * S]
        yhg = area(0, 4, S)
        sgt = area(8192, 16, S)
        mg = area(12288, KC, S)
        mtmp = area(14336, 2, S)
        grow = area(15360, D)
        dg = area(16384, KC, P)
        frow = area(16384, D)
        dg2 = area(17408, KC, P)
        glrow = area(10240, D)
        wre = area(11264, KC, 36)
        brt = area(11600, 36)
        lg36 = area(11700, NT, 36)

        epsc = sm(1)

        class Moe:

            def __init__(self, n, experts, per, U, C, wg, wu, wd, load0):
                self.n, self.experts, self.per, self.U, self.C, self.load0 = n, experts, per, U, C, load0
                self.wg, self.wu, self.wd = wg, wu, wd
                self.E = experts // per
                self.W = per * C
                self.chunks = 4 * self.E * U

            def own(self, c):
                o = self.C * (c // 4 if self.per > 1 else 0)
                return slice(o, o + self.C)

        def moe_sources(moe, g, j):
            e, j = (g, j) if moe.per == 1 else (g * moe.per + j, 0)
            return (moe.wg[e, :, j * UW:(j + 1) * UW].rearrange("(k p) n -> p k n", p=P),
                    moe.wu[e, :, j * UW:(j + 1) * UW].rearrange("(k p) n -> p k n", p=P),
                    moe.wd[e, j * UW:(j + 1) * UW, :].rearrange("(k p) n -> p k n", p=P))

        def cols(name, c0, n=512, k=KC):
            w = ins[name]
            if len(w.shape) == 3:
                w = w[0]
            return w[:, c0:c0 + n].rearrange("(k p) n -> p k n", p=P), k, n

        def rows(name, r0, k):
            w = ins[name]
            if len(w.shape) == 3:
                w = w[0]
            return w[r0:r0 + k * P, :].rearrange("(k p) n -> p k n", p=P), k, D

        plan = [("win%d" % i, *cols("w_in_even", 512 * i), done)
                for i, done in enumerate((("qk_proj", 2), ("qk_proj", 4), ("v_proj", 1), ("xb_proj", 1), ("gb_proj", 1)))]
        plan += [("ada%d" % i, *cols("w_ada_2", 512 * i), ("ada", i + 1)) for i in range(12)]
        plan += [("wout%d" % i, *cols("w_out_even", 512 * i), ("y_ready", i + 1)) for i in range(2)]
        FU = [(u * UW, min(UW, FFN - u * UW)) for u in range(-(-FFN // UW))]
        for u, (f0, n) in enumerate(FU):
            seen = (f0 + n) // P
            plan += [("fg%d" % u, *cols("ffn_wg", f0, n), ("gu_ready", seen)),
                     ("fu%d" % u, *cols("ffn_wu", f0, n), ("gu_ready", seen)),
                     ("fd%d" % u, *rows("ffn_wd", f0, n // P), ("down_done", seen))]
        plan += [("band", ins["k_band"].rearrange("(k p) g t -> p k (g t)", p=P), NT, 4 * S, ("pool_ready", 1))]
        plan += [("poolw", ins["pool_w"][0].rearrange("g (k p) n -> p (g k) n", p=P), 8, S, ("pool_y", 1))]
        while len(plan) % NSLOT:
            plan.append(("pad%d" % len(plan), None, 0, 0, ("down_done", 1)))
        M1 = len(plan)
        moe1 = Moe(1, E1, 1, F1 // UW, C1, ins["moe_wg"][0], ins["moe_wu"][0], ins["moe_wd"][0], M1)
        number = {e[0]: i for i, e in enumerate(plan)}
        COL = {"k": 512, "v": 1024, "q": 0, "zd": 1536, "hq": 2064, "f0": 2576, "hi": 3600, "f1": 3088, "hz": 4112,
               "gd0": 4624, "gd1": 5136, "gh0": 5648, "gh1": 6160}
        READ = {"k": ("k_proj", 4), "v": ("v2_proj", 4), "q": ("q_proj", 1), "zd": ("zd_proj", 1), "hq": ("hq_proj", 1),
                "hi": ("hi_proj", 1), "f0": ("f_proj", 1), "f1": ("f_proj", 2), "hz": ("hz_proj", 1),
                "gd0": ("gate_proj", 1), "gd1": ("gate_proj", 2), "gh0": ("gate_proj", 3), "gh1": ("gate_proj", 4)}
        plan2 = [(n, *cols("w_in_2", c), READ[n]) for n, c in COL.items()]
        plan2 += [("brd", *rows("w_br_dn_2", 0, 4), ("br", 4)), ("brh", *rows("w_br_hg_2", 0, 4), ("br", 8))]
        plan2 += [("wo%d" % i, *cols("w_out_2", 512 * i), ("y2_ready", i + 1)) for i in range(2)]
        while len(plan2) % NSLOT:
            plan2.append(("padb%d" % len(plan2), None, 0, 0, ("y2_ready", 1)))
        P2 = M1 + 3 * moe1.E * moe1.U
        M2 = P2 + len(plan2)
        number.update({e[0]: P2 + i for i, e in enumerate(plan2)})
        moe2 = Moe(2, E2, 2, 2, C2, ins["w_exp_gate_2"][0], ins["w_exp_up_2"][0], ins["w_exp_down_2"][0], M2)

        def entry(i):
            return plan[i] if i < M1 else plan2[i - P2]

        TILE = ((2, 3, 0, 1), (3, 2, 1, 0))

        def p1_count(s_, d, l):
            return 12 * s_ + 2 * (l - 1) + d + 1

        def aoff_count(s_, d, l):
            return 12 * s_ + 2 * (l - 1) + d + 1

        def tu_count(s_, d, l):
            return 14 * s_ + 2 * l + d + 1

        def permuted(ap):
            return ap.rearrange("p (r c) -> p c r", r=4)

        def slot(i, k, n):
            return ring[:, i % NSLOT, 0:k * n].rearrange("p (k n) -> p k n", k=k)

        block = ctx.enter_context(nc.Block())

        @block.sync
        def _(sp):
            def load(i, before):
                _, src, k, n, _ = entry(i)
                if before:
                    sp.wait_ge(*at(before[0], before[1]))
                if src is None:
                    sp.sem_inc(sem("loaded%d" % (i % NSLOT)), 16)
                else:
                    sp.dma_start(slot(i, k, n), src).then_inc(inc("loaded%d" % (i % NSLOT)), 16)

            def load_unit(moe, x, e, j, par, gu, dn):
                for t, src in enumerate(moe_sources(moe, e, j)):
                    need = (gu, gu, dn)[t]
                    if isinstance(need, tuple):
                        sp.wait_ge(*at(need[0], need[1]))
                    elif need is not None:
                        sp.wait_ge(*at("m%d_%s" % (moe.n, "dn" if t == 2 else "gu"), need))
                    s_ = 3 * par + t
                    dst = ring[:, s_, :].rearrange("p (k n) -> p k n", k=KC if t < 2 else 4)
                    sp.dma_start(dst, src).then_inc(inc("%sloaded%d" % ("" if x == "m" else "x%d_" % moe.n, s_)), 16)

            def stream(moe, x, R, first):
                per = 2 * moe.U

                def unit(p, w):
                    v = p * per + w
                    e, j = 2 * p + w // moe.U, w % moe.U
                    load_unit(moe, x, e, j, w % 2, R + 4 * v - 4, R + 4 * v)

                for w in range(per):
                    if w < 2:
                        for t, src in enumerate(moe_sources(moe, w // moe.U, w % moe.U)):
                            s_ = 3 * w + t
                            if first[s_]:
                                sp.wait_ge(*at(first[s_][0], first[s_][1]))
                            dst = ring[:, s_, :].rearrange("p (k n) -> p k n", k=KC if t < 2 else 4)
                            sp.dma_start(dst, src).then_inc(inc("%sloaded%d" % ("" if x == "m" else "x%d_" % moe.n, s_)), 16)
                    else:
                        unit(0, w)
                with sp.Fori(1, moe.E // 2) as p:
                    for w in range(per):
                        unit(p, w)

            def overflow(moe):
                sp.wait_ge(*at("rounds%d_ready" % moe.n, 1))
                N = moe.chunks
                rounds = sp.value_load(rounds_i[moe.n - 1][0:1, 0:1], min_val=1, max_val=8)
                with sp.If(rounds > 1):
                    sp.wait_ge(*at("m%d_dn" % moe.n, N + 4))
                    with sp.Fori(1, rounds) as r:
                        stream(moe, "x", r * N, [None] * NSLOT)
                        sp.wait_ge(*at("m%d_dn" % moe.n, r * N + N + 4))
                        sp.sem_inc(sem("rounds_streamed"), 1)

            before = [None] * NSLOT
            for i in range(len(plan)):
                if i == 1:
                    sp.wait_ge(*at("rows_in", 16 * (len(ROWS_A) + len(ROWS_B))))
                    sp.wait_ge(*at("x_in", 16))
                    sp.wait_ge(*at("table_in", 16))
                load(i, before[i % NSLOT])
                before[i % NSLOT] = plan[i][4]
            stream(moe1, "m", 0, before)
            overflow(moe1)

            def tail_of(moe):
                n = moe.chunks
                g_, d_ = "m%d_gu" % moe.n, "m%d_dn" % moe.n
                return [(g_, n - 4), (g_, n - 4), (d_, n), (g_, n), (g_, n), (d_, n + 4)]

            before = tail_of(moe1)
            for i in range(P2, M2):
                load(i, before[i % NSLOT])
                before[i % NSLOT] = entry(i)[4]
            stream(moe2, "m", 0, before)
            overflow(moe2)
            sp.wait_ge(*at("result", 1))
            sp.dma_start(out[0].rearrange("(t p) d -> p t d", p=P), res[:, :, :]).then_inc(inc("out_stored"), 16)
            sp.wait_ge(*at("out_stored", 16))

        @block.tensor
        def _(pe):
            mm = nc.tensor.matmul

            def take(name):
                i = number[name]
                _, src, k, n, _ = entry(i)
                pe.wait_ge(*at("loaded%d" % (i % NSLOT), 16 * (i // NSLOT + 1)))
                return slot(i, k, n)

            def chain(outp, pairs):
                n = len(pairs)
                for i, (l, r) in enumerate(pairs):
                    last = mm(outp, l, r, start=(i == 0), stop=(i == n - 1))
                return last

            def ada(i):
                if i < 12:
                    w = take("ada%d" % i)
                    if i == 0:
                        pe.wait_ge(*at("c_silu", 1))
                        pe.wait_ge(*at("gb_copied", 1))
                        pe.wait_ge(*at("xb_copied", 1))
                    if i >= 2:
                        pe.wait_ge(*at("mod_row", i - 1))
                    chain(ps[0:2, 5 + i % 2, :], [(scT[:, k, :], w[:, k, :]) for k in range(KC)]).then_inc(inc("ada"), 1)
                if i >= 1:
                    pe.wait_ge(*at("mod_row", i))
                    for m in range(4):
                        o = 2 * (4 * (i - 1) + m)
                        last = nc.tensor.transpose(ps[:, 7, o:o + 2], modrow[0:2, (i - 1) % 2, m * P:(m + 1) * P], ident[0:2, 0:2])
                    last.then_inc(inc("ada_cols"), 1)

            def norm_T(i, x_at=None):
                pe.wait_ge(*at("xn_ready", (i if x_at is None else x_at) + 1))
                for c in range(KC):
                    for t in range(NT):
                        last = nc.tensor.transpose(ps[:, c // 2, (c % 2) * S + t * P:(c % 2) * S + (t + 1) * P],
                                                   xn[:, t, c * P:(c + 1) * P], ident)
                    if c % 2:
                        last.then_inc(inc("xnT_ready"), 1)

            def mlp_up(g, u, j, n, T, hsrc):
                if n >= 4:
                    pe.wait_ge(*at("act_ready", n - 3))
                chain(ps[:, n % 4, 0:T], [(g[:, k, j * P:(j + 1) * P], hsrc[:, k, :]) for k in range(KC)])
                last = chain(ps[:, n % 4, 256:256 + T], [(u[:, k, j * P:(j + 1) * P], hsrc[:, k, :]) for k in range(KC)])
                last.then_inc(inc("gu_ready"), 1)
                return last

            def moe_round(moe, x, R):
                C, U, E = moe.W, moe.U, moe.E
                N = moe.chunks
                nm = "m%d_" % moe.n
                ld = "" if x == "m" else "x%d_" % moe.n
                ld0 = moe.load0 // NSLOT if x == "m" else (R - 1) * (E * U // 2)

                def gather(g, b):
                    pe.wait_ge(*at(nm + "G", R * (E + 1) + g + 1))
                    pe.wait_ge(*at(nm + "added", R * (E + 1) + g))
                    for k in range(KC):
                        chain(ps[:, 2 + k // 4, (k % 4) * C:(k % 4 + 1) * C],
                              [(xnA[:, t, k * P:(k + 1) * P], m_G[:, t, 0:C]) for t in range(NT)])
                    for t in range(NT):
                        last = nc.tensor.transpose(ps[0:C, 6, t * P:(t + 1) * P], m_Gc[:, t, 0:C], ident)
                    last.then_inc(inc(nm + "gath"), 1)

                def scatter(k, b):
                    pe.wait_ge(*at(nm + "y", R * E + k + 1))
                    pe.wait_ge(*at(nm + "gcT", R * (E + 1) + k + 1))
                    pe.wait_ge(*at(nm + "xg", R * (E + 1) + k + 1))
                    for t in range(NT):
                        for c in range(2):
                            last = mm(ps[:, (6 if t == 0 else 2) + c, :], GcT[0:C, 1 - b, t, :], ysb[0:C, c * 512:(c + 1) * 512],
                                      start=True, stop=True)
                        last.then_inc(inc(nm + "scat"), 1)

                def expert(e, b, v, half):
                    par0 = (b * U) % 2
                    n0 = R * N + 4 * v
                    x_ = xgT[:, b, 0:KC * C].rearrange("p (k c) -> p k c", k=KC)
                    pe.wait_ge(*at(nm + "xg", R * (E + 1) + e + 1))

                    def where(c, q):
                        j = c // 4
                        return (par0 + j) % 2, half + q + (par0 + j) // 2

                    def up(c, q=0):
                        par, hf = where(c, q)
                        if c % 4 == 0:
                            for s_ in (3 * par, 3 * par + 1):
                                pe.wait_ge(*at("%sloaded%d" % (ld, s_), (ld0 + hf) * 16 + 16))
                        pe.wait_ge(*at(nm + "act", n0 + 8 * q + c + 3))
                        for half_, s_ in ((0, 3 * par), (1, 3 * par + 1)):
                            w = ring[:, s_, :].rearrange("p (k n) -> p k n", k=KC)
                            last = chain(ps[:, c % 2, 256 * half_:256 * half_ + C],
                                         [(w[:, k, (c % 4) * P:(c % 4 + 1) * P], x_[:, k, :]) for k in range(KC)])
                        last.then_inc(inc(nm + "gu"), 1)

                    def down(c, q=0):
                        par, hf = where(c, q)
                        if c % 4 == 0:
                            pe.wait_ge(*at("%sloaded%d" % (ld, 3 * par + 2), (ld0 + hf) * 16 + 16))
                        pe.wait_ge(*at(nm + "act", n0 + 8 * q + c + 5))
                        w = ring[:, 3 * par + 2, :].rearrange("p (k n) -> p k n", k=4)
                        for h_ in range(2):
                            last = mm(ps[0:C, 4 + h_, :], m_act[:, c % (4 * moe.per), 0:C], w[:, c % 4, h_ * 512:(h_ + 1) * 512],
                                      start=(c == 0), stop=(c == 4 * U - 1))
                        last.then_inc(inc(nm + "dn"), 1)

                    up(0)
                    scatter(e, b)
                    if U == 2:
                        for c in range(7):
                            if c == 6:
                                gather(e + 1, 1 - b)
                            up(c + 1)
                            down(c)
                    else:
                        for c in range(4):
                            up(c + 1)
                            down(c)
                        with pe.Fori(0, (U - 3) // 2) as q:
                            for c in range(4, 12):
                                up(c + 1, q)
                                down(c, q)
                        for c in range(4 * U - 8, 4 * U - 1):
                            if c == 4 * U - 2:
                                gather(e + 1, 1 - b)
                            up(c + 1)
                            down(c)
                    down(4 * U - 1)

                gather(0, 0)
                with pe.Fori(0, E // 2) as p:
                    for b in range(2):
                        expert(2 * p + b, b, 2 * U * p + U * b, U * p + (b * U) // 2)
                scatter(E, 0)

            def routed(moe):
                pe.wait_ge(*at("sel%d_ready" % moe.n, 1))
                E = moe.experts
                mm(ps[:, 7, 0:E], tri_le, seli[:, 0, 0:E], start=True, stop=True)
                chain(ps[:, 7, E:2 * E], [(ones, seli[:, 0, 0:E]), (tri_le, seli[:, 1, 0:E])])
                chain(ps[:, 7, 2 * E:3 * E], [(ones, seli[:, 0, 0:E]), (ones, seli[:, 1, 0:E])]).then_inc(inc("rank%d_sum" % moe.n), 1)
                pe.wait_ge(*at("rounds%d_ready" % moe.n, 1))
                pe.sem_inc(sem("m%d_dn" % moe.n), 4)
                pe.sem_inc(sem("m%d_y" % moe.n), 1)
                moe_round(moe, "m", 0)
                rounds = pe.value_load(rounds_i[moe.n - 1][0:1, 0:1], min_val=1, max_val=8)
                with pe.If(rounds > 1):
                    with pe.Fori(1, rounds) as r:
                        moe_round(moe, "x", r)

            pe.wait_ge(*at("table_in", 16))
            pe.wait_ge(*at("rows_in", 16 * (len(ROWS_A) + len(ROWS_B))))
            nc.tensor.transpose(ps[:, 7, 0:NA], rowsA[0:NA, :], ident[0:NA, 0:NA])
            nc.tensor.transpose(ps[:, 7, 128:128 + NB], rowsB[0:NB, :], ident[0:NB, 0:NB]).then_inc(inc("colsT_ready"), 1)

            norm_T(0)
            pe.wait_ge(*at("hT_ready", 1))
            pe.wait_ge(*at("cols_ready", 1))
            for b, name in ((4, "win0"), (0, "win1")):
                w = take(name)
                for m in range(4):
                    last = chain(ps[:, b + m // 2, (m % 2) * S:(m % 2 + 1) * S],
                                 [(w[:, k, m * P:(m + 1) * P], hTx[:, k, :]) for k in range(KC)])
                    if m % 2:
                        last.then_inc(inc("qk_proj"), 1)
            w = take("win2")
            for t in range(NT):
                last = chain(ps[:, 2 + t, :], [(hTx[:, k, t * P:(t + 1) * P], w[:, k, :]) for k in range(KC)])
            last.then_inc(inc("v_proj"), 1)
            w = take("win3")
            for m in range(4):
                last = chain(ps[:, 6 + m // 2, (m % 2) * S:(m % 2 + 1) * S],
                             [(w[:, k, m * P:(m + 1) * P], hTx[:, k, :]) for k in range(KC)])
            last.then_inc(inc("xb_proj"), 1)
            w = take("win4")
            pe.wait_ge(*at("qk_copied", 2))
            for m in range(4):
                last = chain(ps[:, 4 + m // 2, (m % 2) * S:(m % 2 + 1) * S],
                             [(w[:, k, m * P:(m + 1) * P], hTx[:, k, :]) for k in range(KC)])
            last.then_inc(inc("gb_proj"), 1)
            pe.wait_ge(*at("v_copied", 1))
            pe.wait_ge(*at("table1_in", 16))
            for c in range(8):
                last = mm(ps[:, c // 2, (c % 2) * S:(c % 2 + 1) * S], rot, qk[:, c, :], start=True, stop=True)
            last.then_inc(inc("rot_ready"), 1)
            for qt in range(NT):
                nk = P * (qt + 1)
                pe.wait_ge(*at("rope_done", 1))
                pe.wait_ge(*at("xb_copied", 1))
                pe.wait_ge(*at("gb_copied", 1))
                sb_ = 0
                if qt:
                    pe.wait_ge(*at("o_copied", 2))
                for m in range(2):
                    for h in range(H):
                        last = mm(ps[:, sb_ + 2 * m + h // 2, (h % 2) * S:(h % 2) * S + nk],
                                  qk[64 * m:64 * m + 64, h, qt * P:(qt + 1) * P], qk[64 * m:64 * m + 64, 4 + h, 0:nk],
                                  start=True, stop=True)
                last.then_inc(inc("scores_ready"), 1)
                for i in range(3 * qt, 3 * qt + 3):
                    ada(6 * qt + (i - 3 * qt))
                pe.wait_ge(*at("w_ready", qt + 1))
                for kb in range(qt + 1):
                    for h in range(H):
                        last = nc.tensor.transpose(ps[:, sb_ + kb, h * P:(h + 1) * P], wts[:, h, kb * P:(kb + 1) * P], ident)
                last.then_inc(inc("wT_ready"), 1)
                ada(6 * qt + 3)
                pe.wait_ge(*at("wT_copied", qt + 1))
                for h in range(H):
                    last = chain(ps[:, sb_ + 2, h * P:(h + 1) * P],
                                 [(wT[:, kb, h, :], vtok[:, kb, h * P:(h + 1) * P]) for kb in range(qt + 1)])
                last.then_inc(inc("o_ready"), 1)
                ada(6 * qt + 4)
                ada(6 * qt + 5)
                if qt:
                    ada(12)
                pe.wait_ge(*at("o_normed", qt + 1))
                for h in range(H):
                    last = nc.tensor.transpose(ps[:, sb_ + 3, h * P:(h + 1) * P], ot[:, h, :], ident)
                last.then_inc(inc("oT_ready"), 1)
            pe.wait_ge(*at("xc_ready", 1))
            pe.wait_ge(*at("wgate_in", 16 * 16))
            pe.wait_ge(*at("o_copied", 4))
            for g in range(2):
                for m in range(4):
                    last = mm(ps[:, 2 * g + m // 2, (m % 2) * S:(m % 2 + 1) * S], wgate[:, g, m, :], xc[:, m, :],
                              start=True, stop=True)
            last.then_inc(inc("gates_ready"), 1)
            pe.wait_ge(*at("mod_ready", 1))
            for part in range(2):
                if part:
                    pe.wait_ge(*at("rec_ready", 1))
                for n in range(2):
                    w = take("wout%d" % n)
                    for t in range(NT):
                        for k in range(4 * part, 4 * part + 4):
                            last = mm(ps[:, 4 + 2 * n + t, :], mixT[:, k, t * P:(t + 1) * P], w[:, k, :],
                                      start=(k == 0), stop=(k == KC - 1))
                    if part:
                        last.then_inc(inc("y_ready"), 1)
            norm_T(1)
            pe.wait_ge(*at("hT_ready", 2))
            chunks = [(u, j) for u, (f0, n) in enumerate(FU) for j in range(n // P)]
            for n in range(len(chunks) + 1):
                if n < len(chunks):
                    u, j = chunks[n]
                    if j == 0:
                        g_, u_ = take("fg%d" % u), take("fu%d" % u)
                    last = mlp_up(g_, u_, j, n, S, hTx)
                if n >= 1:
                    u, j = chunks[n - 1]
                    d_ = take("fd%d" % u)
                    pe.wait_ge(*at("act_ready", n))
                    for t in range(NT):
                        for c in range(2):
                            last = mm(ps[:, 4 + 2 * t + c, :], actb[:, (n - 1) % 4, t * P:(t + 1) * P],
                                      d_[:, j, c * 512:(c + 1) * 512], start=(n == 1), stop=(n == len(chunks)))
                    last.then_inc(inc("down_done"), 1)
            pe.wait_ge(*at("xn_ready", 3))
            w = take("band")
            for c in range(KC):
                last = chain(ps[:, c // 2, (c % 2) * S:(c % 2 + 1) * S],
                             [(xn[:, t, c * P:(c + 1) * P], w[:, t, (c // 2) * S:(c // 2 + 1) * S]) for t in range(NT)])
            last.then_inc(inc("pool_ready"), 1)
            pe.wait_ge(*at("poolT_copied", 1))
            w = take("poolw")
            for t in range(NT):
                for g in range(4):
                    last = chain(ps[:, 4 + 2 * t + g // 2, (g % 2) * S:(g % 2 + 1) * S],
                                 [(poolT[:, 2 * g + k, t * P:(t + 1) * P], w[:, 2 * g + k, :]) for k in range(2)])
            last.then_inc(inc("pool_y"), 1)

            norm_T(2, 3)
            pe.wait_ge(*at("hTc_ready", 1))
            norm_T(3, 4)
            pe.wait_ge(*at("hT_ready", 3))
            pe.wait_ge(*at("router1_in", 16))
            for t in range(NT):
                last = chain(ps[:, 6, t * E1:(t + 1) * E1], [(hTx[:, k, t * P:(t + 1) * P], rw1[:, k, :]) for k in range(KC)])
            last.then_inc(inc("logits_ready"), 1)
            routed(moe1)
            w = take("k")
            pe.wait_ge(*at("res_ready", 4))
            for m in range(4):
                chain(ps[:, 4 + m, S:2 * S], [(w[:, k, m * P:(m + 1) * P], hT[:, k, S:2 * S]) for k in range(KC)])
            norm_T(4, 6)
            pe.wait_ge(*at("hT_ready", 4))
            for m in range(4):
                chain(ps[:, 4 + m, 0:S], [(w[:, k, m * P:(m + 1) * P], hTx[:, k, :]) for k in range(KC)])\
                    .then_inc(inc("k_proj"), 1)
            w = take("v")
            for m in range(4):
                chain(ps[:, m, :], [(w[:, k, m * P:(m + 1) * P], hT[:, k, :]) for k in range(KC)])\
                    .then_inc(inc("v2_proj"), 1)
            w = take("q")
            pe.wait_ge(*at("kraw", 1))
            for m in range(4):
                last = chain(ps[:, 4 + m // 2, (m % 2) * S:(m % 2 + 1) * S],
                             [(w[:, k, m * P:(m + 1) * P], hTx[:, k, :]) for k in range(KC)])
            last.then_inc(inc("q_proj"), 1)
            pe.wait_ge(*at("wba_in", 16))
            for t in range(4):
                last = chain(ps[:, 6, t * 16:(t + 1) * 16], [(hT[:, k, t * P:(t + 1) * P], wba[:, k, :]) for k in range(KC)])
            last.then_inc(inc("ba_proj"), 1)
            pe.wait_ge(*at("k_sq", 1))
            pe.wait_ge(*at("vraw", 1))
            for h in range(H):
                last = mm(ps[:, h, :], ones, sq[:, h, :], start=True, stop=True)
            last.then_inc(inc("k_ss"), 1)
            pe.wait_ge(*at("gdec_ready", 1))
            for t in range(4):
                mm(ps[:, 7, t * 8:t * 8 + 4], tri_le, gdec[:, t, 0:4], start=True, stop=True)
                last = mm(ps[:, 7, t * 8 + 4:t * 8 + 8], tri_ge, gdec[:, t, 4:8], start=True, stop=True)
            last.then_inc(inc("gcs_sum"), 1)
            pe.wait_ge(*at("kF_ready", 1))
            for t in range(4):
                for h in range(H):
                    last = nc.tensor.transpose(ps[:, t, h * P:(h + 1) * P], kF[:, h, t * P:(t + 1) * P], ident)
            last.then_inc(inc("kT_ready"), 1)
            pe.wait_ge(*at("vc_ready", 1))
            pe.wait_ge(*at("qraw", 1))
            pe.wait_ge(*at("ba_read", 1))
            pe.wait_ge(*at("gcs_ready", 1))
            for t in range(4):
                for h in range(H):
                    last = nc.tensor.transpose(ps[:, 4 + t, h * P:(h + 1) * P], vc[:, h, t * P:(t + 1) * P], ident)
            last.then_inc(inc("vT_ready"), 1)
            pe.wait_ge(*at("kTok_ready", 1))
            pe.wait_ge(*at("q_sq", 1))
            for i in range(2):
                last = mm(ps[:, i, :], ones, sq[:, 2 * i:2 * i + 2, 0:S], start=True, stop=True)
            last.then_inc(inc("q_ss"), 1)
            pe.wait_ge(*at("qF_ready", 1))
            pe.wait_ge(*at("vTok_ready", 1))
            for s_ in range(4):
                x_part = s_ >= 2
                for d in range(2):
                    n, b = 2 * s_ + d, 4 * d
                    t = TILE[d][s_]
                    tri = (tri_le, tri_ge)[d]
                    if s_:
                        pe.wait_ge(*at("S_ready", n - 1))
                    for h in range(H):
                        kf = kF[:, h, t * P:(t + 1) * P]
                        mm(ps[:, b, h * P:(h + 1) * P], kf, kf, start=True, stop=True)
                    for h in range(H):
                        last = mm(ps[:, b + 1, h * P:(h + 1) * P], gdec[:, t, 4 * d + h:4 * d + h + 1].to_broadcast([P, P]), tri,
                                  start=True, stop=True)
                    if x_part:
                        for h in range(H):
                            last = mm(ps[:, b + 2, h * P:(h + 1) * P], kF[:, h, t * P:(t + 1) * P], qF[:, h, t * P:(t + 1) * P],
                                      start=True, stop=True)
                    last.then_inc(inc("gram"), 1)
                for d in range(2):
                    n, b = 2 * s_ + d, 4 * d
                    A = WK[d][0]
                    pe.wait_ge(*at("A_ready", n + 1))
                    for h in range(H):
                        last = nc.tensor.transpose(ps[:, b, h * P:(h + 1) * P], A[:, h, :], ident)
                    last.then_inc(inc("At_ready"), 1)
                for l in range(1, len(LEVELS)):
                    for d in range(2):
                        m = (2 * s_ + d) * 6 + l
                        pe.wait_ge(*at("Aoff_ready", aoff_count(s_, d, l)))
                        pe.wait_ge(*at("TU_ready", tu_count(s_, d, l - 1)))
                        if l == 1:
                            pe.wait_ge(*at("A_ready", 2 * s_ + d + 1))
                            if x_part:
                                pe.wait_ge(*at("attT_dn", 2 * (s_ - 2) + d + 1))
                            pe.wait_ge(*at("eR", 2 * s_ + d + 1))
                        Ao, T = WK[d][2 + l % 2], WK[d][4]
                        for h in range(H):
                            last = mm(ps[:, 4 * d + 1, h * P:(h + 1) * P], Ao[:, h, :], T[:, h, :], start=True, stop=True)
                        last.then_inc(inc("P1_ready"), 1)
                    for d in range(2):
                        pe.wait_ge(*at("P1_copied", p1_count(s_, d, l)))
                        P1, U, T = WK[d][6], WK[d][5], WK[d][4]
                        if l < len(LEVELS) - 1:
                            for h in range(H):
                                mm(ps[:, 4 * d + 2, h * P:(h + 1) * P], U[:, h, :], P1[:, h, :], start=True, stop=True)
                        for h in range(H):
                            last = mm(ps[:, 4 * d + 3, h * P:(h + 1) * P], P1[:, h, :], U[:, h, :], start=True, stop=True)
                        last.then_inc(inc("TU_step"), 1)
                for d in range(2):
                    n, b = 2 * s_ + d, 4 * d
                    U, kbg, nw, vb = WK[d][5], WK[d][6], WK[d][2], WK[d][3]
                    pe.wait_ge(*at("TU_ready", tu_count(s_, d, 6)))
                    pe.wait_ge(*at("kbg_ready", n + 1))
                    for h in range(H):
                        last = mm(ps[:, b + 1, h * P:(h + 1) * P], kbg[:, h, :], U[:, h, :], start=True, stop=True)
                    last.then_inc(inc("wT_dn"), 1)
                for d in range(2):
                    n, b = 2 * s_ + d, 4 * d
                    U, nw, vb = WK[d][5], WK[d][2], WK[d][3]
                    pe.wait_ge(*at("nw_ready", n + 1))
                    for h in range(H):
                        pairs = [(U[:, h, :], vb[:, h, :])]
                        if s_:
                            pairs.append((nw[:, h, :], Sd[d][:, h, :]))
                        last = chain(ps[:, b + 2, h * P:(h + 1) * P], pairs)
                    last.then_inc(inc("vnew"), 1)
                for d in range(2):
                    n, b = 2 * s_ + d, 4 * d
                    vn, kd, qe_, at_ = WK[d][4], WK[d][1], WK[d][7], WK[d][8]
                    pe.wait_ge(*at("vn_ready", n + 1))
                    if x_part:
                        for h in range(H):
                            last = chain(ps[:, b + 3, h * P:(h + 1) * P], [(Sd[d][:, h, :], qe_[:, h, :]), (vn[:, h, :], at_[:, h, :])])
                    for h in range(H):
                        last = mm(ps[:, b, h * P:(h + 1) * P], kd[:, h, :], vn[:, h, :], start=True, stop=True)
                    last.then_inc(inc("dS_ready"), 1)
            w = take("zd")
            pe.wait_ge(*at("S_ready", 8))
            for m in range(4):
                last = chain(ps[:, m // 2, (m % 2) * S:(m % 2 + 1) * S],
                             [(w[:, k, m * P:(m + 1) * P], hTx[:, k, :]) for k in range(KC)])
            last.then_inc(inc("zd_proj"), 1)
            pe.wait_ge(*at("o_sq", 1))
            for i in range(2):
                last = mm(ps[:, 2 + i, :], ones, rs[:, 2 * i:2 * i + 2, :], start=True, stop=True)
            last.then_inc(inc("o_ss"), 1)
            w = take("hq")
            for m in range(4):
                last = chain(ps[:, 4 + m // 2, (m % 2) * S:(m % 2 + 1) * S],
                             [(w[:, k, m * P:(m + 1) * P], hTx[:, k, :]) for k in range(KC)])
            last.then_inc(inc("hq_proj"), 1)
            for d in range(2):
                w = take("f%d" % d)
                if d == 0:
                    pe.wait_ge(*at("hq_ready", 1))
                else:
                    pe.wait_ge(*at("att_masked", 8))
                for m in range(4):
                    last = chain(ps[:, 4 + m, :], [(w[:, k, m * P:(m + 1) * P], hT[:, k, :]) for k in range(KC)])
                last.then_inc(inc("f_proj"), 1)
                if d == 0:
                    w = take("hi")
                    pe.wait_ge(*at("rs_done", 1))
                    pe.wait_ge(*at("hxp_ready", 1))
                    for t in range(4):
                        def tok(k):
                            if t < NT:
                                return hxp[:, k, t * P:(t + 1) * P]
                            return hT[:, k, t * P:(t + 1) * P]
                        last = chain(ps[:, t, :], [(tok(k), w[:, k, :]) for k in range(KC)])
                    last.then_inc(inc("hi_proj"), 1)
                else:
                    pe.wait_ge(*at("f_sig", 2))
                    for b, name in ((4, "hz"), (6, "gd0")):
                        w = take(name)
                        for m in range(4):
                            last = chain(ps[:, b + m // 2, (m % 2) * S:(m % 2 + 1) * S],
                                         [(w[:, k, m * P:(m + 1) * P], hTx[:, k, :]) for k in range(KC)])
                        last.then_inc(inc("hz_proj" if b == 4 else "gate_proj"), 1)
                    pe.wait_ge(*at("og_ready", 1))
                pe.wait_ge(*at("kd_ready", d + 1))
                pe.wait_ge(*at("hv_ready", 1))
                for t in range(NT):
                    for h in range(H):
                        last = nc.tensor.transpose(ps[:, t, h * P:(h + 1) * P], Wd[:, h, t * P:(t + 1) * P], ident)
                last.then_inc(inc("kdT_ready"), 1)
                pe.wait_ge(*at("kdTok_ready", d + 1))
                for h in range(H):
                    last = chain(ps[:, 2, h * P:(h + 1) * P], [(kdTok[:, t, h, :], hv[:, 2 + t, h * P:(h + 1) * P]) for t in range(NT)])
                last.then_inc(inc("Sg_sum"), 1)
                for l in range(8):
                    b = 4 + 2 * (l % 2)
                    n = 8 * d + l
                    if d == 1 and l < 2:
                        pe.wait_ge(*(at("z_silu", 2) if l == 0 else at("gate_sig", 1)))
                    if l == 0:
                        kx, qx = kk, hq
                        pe.wait_ge(*at("kk_ready", d + 1))
                    else:
                        kx, qx = kW, qW
                        pe.wait_ge(*at("W_ready", 8 * d + l))
                    if l >= 2:
                        pe.wait_ge(*at("att_masked", n - 1))
                    for t in range(NT):
                        for h in range(H):
                            last = mm(ps[:, b + t, h * P:(h + 1) * P], kx[:, h, t * P:(t + 1) * P], qx[:, h, t * P:(t + 1) * P],
                                      start=True, stop=True)
                    last.then_inc(inc("att_ready"), 1)
                pe.wait_ge(*at("W_ready", 8 * d + 8))
                pe.wait_ge(*at("Sg_ready", d + 1))
                qt, kt = (1, 0) if d == 0 else (0, 1)
                for h in range(H):
                    last = mm(ps[:, 3, h * P:(h + 1) * P], kW[:, h, kt * P:(kt + 1) * P], qW[:, h, qt * P:(qt + 1) * P],
                              start=True, stop=True)
                last.then_inc(inc("attX_sum"), 1)
                pe.wait_ge(*at("attX_ready", d + 1))
                pe.wait_ge(*at("att_sum", 8 * d + 8))
                pe.wait_ge(*at("qe_ready", d + 1))
                for t in range(NT):
                    for h in range(H):
                        pairs = [(hv[:, t, h * P:(h + 1) * P], attT[:, t, h, :]), (Sg[:, h, :], qe[:, h, t * P:(t + 1) * P])]
                        if t == qt:
                            pairs.append((hv[:, kt, h * P:(h + 1) * P], attX[:, h, :]))
                        last = chain(ps[:, t, h * P:(h + 1) * P], pairs)
                last.then_inc(inc("og_sum"), 1)
            pe.wait_ge(*at("og_ready", 2))
            pe.wait_ge(*at("o_sq", 2))
            for i in range(2):
                last = mm(ps[:, 6 + i, :], ones, rs[:, 2 * i:2 * i + 2, :], start=True, stop=True)
            last.then_inc(inc("o_ss"), 1)
            for i, name in ((1, "gd1"), (2, "gh0"), (3, "gh1")):
                w = take(name)
                if i >= 3:
                    pe.wait_ge(*at("gate_sig", i - 1))
                for m in range(4):
                    last = chain(ps[:, 2 * (i % 2) + m // 2, (m % 2) * S:(m % 2 + 1) * S],
                                 [(w[:, k, m * P:(m + 1) * P], hTx[:, k, :]) for k in range(KC)])
                last.then_inc(inc("gate_proj"), 1)
            pe.wait_ge(*at("rs_done", 2))
            for i, (name, y) in enumerate((("brd", oF), ("brh", yhg))):
                w = take(name)
                pe.wait_ge(*at("y_gated", i + 1))
                for c in range(4):
                    if i:
                        pe.wait_ge(*at("br_read", c + 1))
                    for m in (2 * c, 2 * c + 1):
                        last = chain(ps[:, 4 + c, (m % 2) * S:(m % 2 + 1) * S],
                                     [(w[:, k, m * P:(m + 1) * P], y[:, k, :]) for k in range(4)])
                    last.then_inc(inc("br"), 1)
            pe.wait_ge(*at("dg_ready", 1))
            pe.wait_ge(*at("gate_sig", 4))
            for i in range(2):
                last = mm(ps[:, i, :], ones, dg[:, 4 * i:4 * i + 4, :], start=True, stop=True)
            last.then_inc(inc("grow_sum"), 1)
            pe.wait_ge(*at("mg_ready", 1))
            for n in range(2):
                w = take("wo%d" % n)
                for t in range(NT):
                    last = chain(ps[:, 4 + 2 * n + t, :], [(mg[:, k, t * P:(t + 1) * P], w[:, k, :]) for k in range(KC)])
                last.then_inc(inc("y2_ready"), 1)
            pe.wait_ge(*at("grow_ready", 1))
            pe.wait_ge(*at("dg_ready", 2))
            norm_T(5, 7)
            for i in range(2):
                last = mm(ps[:, 4 + i, :], ones, dg2[:, 4 * i:4 * i + 4, :], start=True, stop=True)
            last.then_inc(inc("grow_sum"), 1)
            pe.wait_ge(*at("hT_ready", 5))
            pe.wait_ge(*at("router2_in", 64))
            for t in range(NT):
                last = chain(ps[:, 6, t * 36:(t + 1) * 36], [(hTx[:, k, t * P:(t + 1) * P], wre[:, k, :]) for k in range(KC)])
            last.then_inc(inc("logits_ready"), 1)
            routed(moe2)

        @block.vector
        def _(ve):
            V = nc.vector

            def done(ins_, name="ve_step"):
                count[name] = count.get(name, 0) + 1
                ins_.then_inc(inc(name), 1)
                ve.wait_ge(*at(name, count[name]))

            def norm(i, src=res):
                ve.wait_ge(*at("sumsq", i + 1))
                done(V.tensor_scalar(ms, ss, 1.0 / D, EPS, ALU.mult, ALU.add), "ms_ready")
                ve.wait_ge(*at("rstd_ready", i + 1))
                for t in range(NT):
                    last = V.tensor_scalar(xn[:, t, :], src[:, t, :], rstd[:, t:t + 1], None, ALU.mult)
                done(last, "xn_ready")

            def norm_copy(i, gain):
                for b in range(4):
                    ve.wait_ge(*at("xnT_ready", 4 * nT[0] + b + 1))
                    last = V.tensor_tensor(hTx[:, 2 * b:2 * b + 2, :], bank(b, 2, S), over(gain[:, 2 * b:2 * b + 2], S), ALU.mult)
                nT[0] += 1
                done(last, "hT_ready")

            nT = [0]

            def norm_modulate(dst, gain, shift, name):
                for c in range(KC):
                    ve.wait_ge(*at("xnT_ready", 4 * nT[0] + c // 2 + 1))
                    last = V.tensor_scalar(dst[:, c, :], ps[:, c // 2, (c % 2) * S:(c % 2 + 1) * S], gain[:, c:c + 1],
                                           shift[:, c:c + 1], ALU.mult, ALU.add)
                nT[0] += 1
                done(last, name)

            def top(E, lg_, m, oh):
                done(V.tensor_reduce(m, lg_, AX.X, ALU.max))
                done(V.tensor_tensor(oh, lg_, over(m, E), ALU.is_equal))
                done(V.scalar_tensor_tensor(oh, oh, -64.0, iota[:, None, 0:E].to_broadcast([P, NT, E]), ALU.mult, ALU.add))
                done(V.tensor_reduce(i1_, oh, AX.X, ALU.min))
                done(V.tensor_tensor(oh, oh, over(i1_, E), ALU.is_equal))

            def route(moe, lg_, scale):
                E, C = moe.experts, moe.C
                o1, o2, s_ = oh1[:, :, 0:E], oh2[:, :, 0:E], seli[:, :, 0:E]
                top(E, lg_, mx1, o1)
                l2 = lgm[:, :, 0:E]
                done(V.scalar_tensor_tensor(l2, o1, -BIG, lg_, ALU.mult, ALU.add))
                top(E, l2, mx2, o2)
                done(V.tensor_tensor(s_, o1, o2, ALU.add), "sel%d_ready" % moe.n)
                done(V.tensor_tensor(dm, mx2, mx1, ALU.subtract), "top%d_diff" % moe.n)
                ve.wait_ge(*at("top%d_exp" % moe.n, 1))
                done(V.tensor_scalar(g1_, e2_, 1.0, None, ALU.add))
                done(V.reciprocal(g1_, g1_))
                if scale is not None:
                    done(V.tensor_tensor(g1_, g1_, scale, ALU.mult))
                done(V.tensor_tensor(g2_, e2_, g1_, ALU.mult))
                done(V.tensor_tensor(o1, o1, over(g1_, E), ALU.mult))
                done(V.tensor_tensor(o2, o2, over(g2_, E), ALU.mult))
                V.memset(comb[:, :, E:E + moe.per], 0.0)
                V.memset(rank[:, :, E:E + moe.per], -1.0)
                done(V.tensor_tensor(comb[:, :, 0:E], o1, o2, ALU.add))
                ve.wait_ge(*at("rank%d_sum" % moe.n, 1))
                done(V.tensor_reduce(cmax, ps[:, 7, 2 * E:3 * E], AX.X, ALU.max))
                done(V.tensor_scalar(rnd, cmax, float(C), 1.0, ALU.is_gt, ALU.add))
                for k in range(2, -(-S // C)):
                    done(V.tensor_scalar(rndt, cmax, float(k * C), None, ALU.is_gt))
                    done(V.tensor_tensor(rnd, rnd, rndt, ALU.add))
                done(V.tensor_tensor(rank[:, :, 0:E], ps[:, 7, 0:2 * E].rearrange("p (t e) -> p t e", t=NT), s_, ALU.mult))
                done(V.tensor_scalar(rank[:, :, 0:E], rank[:, :, 0:E], -1.0, None, ALU.add))
                done(V.memset(ysb, 0.0))
                done(V.memset(GcT[:, 1, :, :], 0.0))
                done(V.tensor_copy(rounds_i[moe.n - 1][:, :], rnd), "rounds%d_ready" % moe.n)

            def moe_round(moe, x, R, acc, copy):
                C, U, E, W, per = moe.C, moe.U, moe.E, moe.W, moe.per
                N = moe.chunks
                nm = "m%d_" % moe.n

                def select(g):
                    for t in range(NT):
                        for j in range(per):
                            o, e = C * j, (slice(per * g + j, per * g + j + 1) if isinstance(g, int) else bass.ds(per * g + j, 1))
                            V.tensor_scalar(m_G[:, t, o:o + C], iota[:, 0:C], rank[:, t, e], None, ALU.is_equal)
                            last = V.tensor_scalar(m_Gc[:, t, o:o + C], iota[:, 0:C], rank[:, t, e], comb[:, t, e], ALU.is_equal, ALU.mult)
                    last.then_inc(inc(nm + "G"), 1)

                def gathered(g, b):
                    ve.wait_ge(*at(nm + "gath", R * (E + 1) + g + 1))
                    copy(xgT[:, b, 0:KC * W].rearrange("p (k c) -> p k c", k=KC)).then_inc(inc(nm + "xg"), 1)

                def act(n, c):
                    i, own = c % (4 * per), moe.own(c)
                    ve.wait_ge(*at(nm + "sg", n + 1))
                    ve.wait_ge(*at(nm + "dn", n + 1))
                    V.tensor_tensor(m_act[:, i, own], m_sg[:, i, own], ps[:, i % 2, 256 + own.start:256 + own.stop], ALU.mult)\
                        .then_inc(inc(nm + "act"), 1)

                def add(k):
                    for t in range(NT):
                        ve.wait_ge(*at(nm + "scat", (R * (E + 1) + k) * 2 + t + 1))
                        for c in range(2):
                            last = V.tensor_tensor(acc[:, t, c * 512:(c + 1) * 512], acc[:, t, c * 512:(c + 1) * 512],
                                                   ps[:, (6 if t == 0 else 2) + c, :], ALU.add)
                    last.then_inc(inc(nm + "added"), 1)

                select(0)
                gathered(0, 0)
                with ve.Fori(0, E // 2) as p:
                    for b in range(2):
                        e = 2 * p + b
                        n0 = R * N + 4 * U * e
                        select(e + 1)
                        act(n0, 0)
                        add(e)
                        for c in range(1, 4 * per):
                            act(n0 + c, c)
                        if per == 1:
                            with ve.Fori(1, U) as j:
                                for c in range(4):
                                    act(n0 + 4 * j + c, c)
                        gathered(e + 1, 1 - b)
                add(E)

            def routed(moe, acc, copy):
                done(V.memset(m_act, 0.0))
                ve.sem_inc(sem("m%d_act" % moe.n), 4)
                moe_round(moe, "m", 0, acc, copy)
                ve.wait_ge(*at("m%d_added" % moe.n, moe.E + 1))
                rounds = ve.value_load(rounds_i[moe.n - 1][0:1, 0:1], min_val=1, max_val=8)
                with ve.If(rounds > 1):
                    with ve.Fori(1, rounds) as r:
                        V.tensor_scalar(rank[:, :, 0:moe.experts + moe.per], rank[:, :, 0:moe.experts + moe.per], -float(moe.C), None, ALU.add).then_inc(inc("x%d_rank" % moe.n), 1)
                        V.memset(ysb, 0.0).then_inc(inc("x%d_rank" % moe.n), 1)
                        ve.wait_ge(*at("x%d_rank" % moe.n, 2 * r))
                        moe_round(moe, "x", r, acc, copy)
                        ve.wait_ge(*at("m%d_added" % moe.n, (r + 1) * (moe.E + 1)))
                        ve.sem_inc(sem("rounds_added"), 1)

            done(V.memset(epsc, EPS), "eps_ready")
            ve.wait_ge(*at("colsT_ready", 1))
            V.tensor_copy(pA[:, :], ps[:, 7, 0:NA])
            done(V.tensor_copy(pB[:, :], ps[:, 7, 128:128 + NB]), "cols_ready")
            ve.wait_ge(*at("lam_in", 64))
            done(V.tensor_tensor(lamv[:, 0:2, :], lamv[:, 0:2, :], lamv[:, 2:4, :], ALU.mult))
            done(V.tensor_reduce(lams[:, 0:2], lamv[:, 0:2, :], AX.X, ALU.add), "lam_dot")
            ve.wait_ge(*at("lam_exp", 1))
            done(V.tensor_tensor(lams[:, 4:5], lams[:, 3:4], lams[:, 2:3], ALU.subtract))
            LAM_INIT = 0.8 - 0.6 * math.exp(-0.3 * 0)
            done(V.tensor_scalar(lams[:, 5:6], lams[:, 4:5], 1.0, -LAM_INIT, ALU.mult, ALU.add))
            ve.wait_ge(*at("nl_ln", 1))
            done(V.tensor_scalar(nl3, colA("rg_lam", 0, 4), -1.0, 0.0, ALU.mult, ALU.max))
            done(V.tensor_tensor(nl3, nl3, nl2, ALU.add))
            done(V.tensor_scalar(nl3, nl3, -8.0, None, ALU.mult), "nl_ready")

            norm(0)
            norm_copy(0, colA("ln_mix_even", 0, 8))
            for i, b in enumerate((4, 5, 0, 1)):
                ve.wait_ge(*at("qk_proj", i + 1))
                done(V.tensor_copy(qk[:, 2 * i:2 * i + 2, :], bank(b, 2, S)), "qk_copied")
            ve.wait_ge(*at("v_proj", 1))
            V.tensor_copy(vtok[:, 0, :], ps[:, 2, :])
            done(V.tensor_copy(vtok[:, 1, :], ps[:, 3, :]), "v_copied")
            ve.wait_ge(*at("xb_proj", 1))
            done(V.memset(xpad[:, :, 0:3], 0.0))
            V.tensor_copy(xpad[:, 0:2, 3:], bank(6, 2, S))
            done(V.tensor_copy(xpad[:, 2:4, 3:], bank(7, 2, S)), "xb_copied")
            for c in range(4):
                last = V.tensor_scalar(xc[:, c, :], xpad[:, c, 3:3 + S], colA("conv_w", 12 + c), colA("conv_b", c), ALU.mult, ALU.add)
            done(last)
            for tap in range(3):
                for c in range(4):
                    last = V.scalar_tensor_tensor(xc[:, c, :], xpad[:, c, tap:tap + S], colA("conv_w", 4 * tap + c),
                                                  xc[:, c, :], ALU.mult, ALU.add)
                done(last, "ve_step" if tap < 2 else "xc_ready")
            ve.wait_ge(*at("rot_ready", 1))
            for b in range(4):
                done(V.tensor_tensor(rtmp, bank(b, 2, S), rep(sinT, 2), ALU.mult))
                done(V.tensor_tensor(qk[:, 2 * b:2 * b + 2, :], qk[:, 2 * b:2 * b + 2, :], rep(cosT, 2), ALU.mult))
                done(V.tensor_tensor(qk[:, 2 * b:2 * b + 2, :], qk[:, 2 * b:2 * b + 2, :], rtmp, ALU.add),
                     "ve_step" if b < 3 else "rope_done")
            for qt in range(NT):
                nk = P * (qt + 1)
                mk = amask[:, P:2 * P] if qt == 0 else amask[:, :]
                ve.wait_ge(*at("scores_ready", qt + 1))
                for b in range(4):
                    last = V.tensor_tensor(sc[:, 2 * b:2 * b + 2, 0:nk], bank(b, 2, S)[:, :, 0:nk], rep(mk, 2), ALU.add)
                done(last)
                done(V.tensor_reduce(mx, sc[:, :, 0:nk], AX.X, ALU.max))
                done(V.tensor_tensor(sc[:, :, 0:nk], sc[:, :, 0:nk], over(mx, nk), ALU.subtract), "s_shifted")
                ve.wait_ge(*at("s_exp", qt + 1))
                done(V.tensor_reduce(smx, sc[:, :, 0:nk], AX.X, ALU.add))
                done(V.reciprocal(rsm, smx))
                done(V.tensor_scalar(rsm[:, 4:8], rsm[:, 4:8], lams[:, 5:6], None, ALU.mult))
                done(V.tensor_tensor(sc[:, :, 0:nk], sc[:, :, 0:nk], over(rsm, nk), ALU.mult))
                done(V.tensor_tensor(wts[:, :, 0:nk], sc[:, 0:4, 0:nk], sc[:, 4:8, 0:nk], ALU.add), "w_ready")
                ve.wait_ge(*at("wT_ready", qt + 1))
                for kb in range(qt + 1):
                    last = V.tensor_copy(wT[:, kb, :, :], bank(kb, 4, P))
                done(last, "wT_copied")
                ve.wait_ge(*at("o_ready", qt + 1))
                done(V.tensor_copy(ot, bank(2, 4, P)), "o_copied")
                done(V.tensor_tensor(osq, ot, ot, ALU.mult))
                done(V.tensor_reduce(o4, osq, AX.X, ALU.add))
                done(V.tensor_scalar(o4b, o4, 1.0 / P, SUB_EPS, ALU.mult, ALU.add), "o_ms")
                ve.wait_ge(*at("o_rstd", qt + 1))
                done(V.tensor_scalar(o4c, o4c, 1.0 - LAM_INIT, None, ALU.mult))
                done(V.tensor_tensor(ot, ot, over(o4c, P), ALU.mult), "o_normed")
                ve.wait_ge(*at("oT_ready", qt + 1))
                done(V.tensor_scalar(mixT[:, 0:4, qt * P:(qt + 1) * P], bank(3, 4, P), colA("subln_g"), None, ALU.mult), "o_copied")
            ve.wait_ge(*at("ada_cols", 12))
            done(V.tensor_tensor(mod, ps[:, 7, 0:96].rearrange("p (a b) -> p a b", a=48), over(colB("b_ada_2", 0, 48), 2), ALU.add), "mod_ready")
            for g_, name, row in ((gA, "g_mix_2", 8), (gM, "g_ffn_2", 32)):
                done(V.scalar_tensor_tensor(g_, mod[:, row:row + 8, 0], 1.0, colB(name, 0, 8), ALU.add, ALU.mult))
            done(V.scalar_tensor_tensor(gC, mod[:, 8:16, 1], 1.0, colB("g_mix_2", 0, 8), ALU.add, ALU.mult))
            ve.wait_ge(*at("gb_copied", 1))
            done(V.tensor_tensor(gt, gbF, gbF, ALU.mult))
            done(V.tensor_scalar(gt, gt, 0.044715, 1.0, ALU.mult, ALU.add))
            done(V.tensor_tensor(gt, gt, gbF, ALU.mult), "gelu_in")
            ve.wait_ge(*at("rg_sig", 1))
            done(V.tensor_tensor(rg_r, rg_r, over(nl3, S), ALU.mult), "log_a")
            done(V.tensor_tensor(rg_i, rg_i, xc, ALU.mult))
            ve.wait_ge(*at("rg_exp", 1))
            done(V.tensor_tensor(rg_u, rg_a, rg_a, ALU.mult))
            done(V.scalar_tensor_tensor(rg_u, rg_u, 1.0, rg_r, ALU.add, ALU.mult))
            done(V.tensor_scalar(rg_u, rg_u, -1.0, 0.0, ALU.mult, ALU.max), "one_minus")
            ve.wait_ge(*at("rg_sqrt", 1))
            done(V.tensor_tensor(rg_u, rg_u, rg_i, ALU.mult))
            for c in range(4):
                last = V.tensor_tensor_scan(rg_h[:, c, :], rg_a[:, c, :], rg_u[:, c, :], 0.0, ALU.mult, ALU.add)
            done(last)
            ve.wait_ge(*at("gelu_tanh", 1))
            done(V.scalar_tensor_tensor(gel, gel, 1.0, gbF, ALU.add, ALU.mult))
            done(V.scalar_tensor_tensor(mixT[:, 4:8, :], rg_h, 0.5, gel, ALU.mult, ALU.mult), "rec_ready")
            for n in range(2):
                ve.wait_ge(*at("y_ready", n + 1))
                for t in range(NT):
                    last = V.tensor_tensor(res[:, t, n * 512:(n + 1) * 512], res[:, t, n * 512:(n + 1) * 512],
                                           ps[:, 4 + 2 * n + t, :], ALU.add)
            done(last, "res_ready")
            norm(1)
            norm_copy(1, colA("ln_ffn_even", 0, 8))
            NFC = FFN // P
            for n in range(NFC):
                ve.wait_ge(*at("sg_ready", n + 1))
                if n >= 4:
                    ve.wait_ge(*at("down_done", n - 3))
                V.tensor_tensor(actb[:, n % 4, :], sgb[:, n % 4, :], ps[:, n % 4, 256:512], ALU.mult).then_inc(inc("act_ready"), 1)
            ve.wait_ge(*at("down_done", NFC))
            for t in range(NT):
                for c in range(2):
                    last = V.tensor_tensor(res[:, t, c * 512:(c + 1) * 512], res[:, t, c * 512:(c + 1) * 512],
                                           ps[:, 4 + 2 * t + c, :], ALU.add)
            done(last, "res_ready")
            norm(2)
            ve.wait_ge(*at("pool_ready", 1))
            for b in range(4):
                last = V.tensor_tensor(poolT[:, 2 * b:2 * b + 2, :], bank(b, 2, S),
                                       over(colA("ln_mix_odd", 2 * b, 2), S), ALU.mult)
            done(last, "poolT_copied")
            ve.wait_ge(*at("pool_scale_in", 16))
            ve.wait_ge(*at("pool_y", 1))
            for t in range(NT):
                for c in range(2):
                    last = V.tensor_tensor(ps[:, 4 + 2 * t + c, :], ps[:, 4 + 2 * t + c, :], brow[:, c * 512:(c + 1) * 512], ALU.mult)
            done(last)
            for t in range(NT):
                for c in range(2):
                    last = V.tensor_tensor(res[:, t, c * 512:(c + 1) * 512], res[:, t, c * 512:(c + 1) * 512],
                                           ps[:, 4 + 2 * t + c, :], ALU.add)
            done(last, "res_ready")
            ve.wait_ge(*at("ctx_in", 16))
            norm(3, cres)
            norm_modulate(hTc, gC, mod[:, 0:8, 1], "hTc_ready")
            norm(4)
            norm_copy(2, colA("ln_ffn_odd", 0, 8))
            ve.wait_ge(*at("logits_ready", 1))
            done(V.tensor_copy(lgt[:, :, 0:E1], ps[:, 6, 0:NT * E1].rearrange("p (t e) -> p t e", t=NT)))
            route(moe1, lgt[:, :, 0:E1], None)
            gain = colA("ln_ffn_odd", 0, 8)

            def copy1(x_):
                C = moe1.W
                for b in range(2):
                    last = V.tensor_tensor(x_[:, 4 * b:4 * b + 4, :], bank(2 + b, 4, C), over(gain[:, 4 * b:4 * b + 4], C), ALU.mult)
                return last

            routed(moe1, res, copy1)
            done(V.memset(lams[:, 7:8], 0.0), "res_ready")
            norm(5)
            ve.wait_ge(*at("fgrow_in", 16))
            for t in range(NT):
                last = V.tensor_tensor(res[:, t, :], xn[:, t, :], fgrow, ALU.mult)
            done(last, "res_ready")
            norm(6)
            norm_modulate(hTx, gA, mod[:, 0:8, 0], "hT_ready")
            V.memset(xraw[:, :, :, 0:1], 0.0)
            done(V.memset(xraw[:, :, :, S + 1:S + 2], 0.0))

            def conv(dst, c0, n):
                for m in range(4):
                    last = V.tensor_scalar(dst(m), xraw[:, m, 0:n, 0:S], colB("dn_conv_2", c0 + m), None, ALU.mult)
                done(last)
                for tap in (1, 2):
                    for m in range(4):
                        last = V.scalar_tensor_tensor(dst(m), xraw[:, m, 0:n, tap:tap + S], colB("dn_conv_2", 12 * tap + c0 + m),
                                                      dst(m), ALU.mult, ALU.add)
                    if tap == 1:
                        done(last)
                return last

            def halves(buf):
                return lambda m: buf[:, m, :].rearrange("p (a b) -> p a b", a=2)

            for m in range(4):
                ve.wait_ge(*at("k_proj", m + 1))
                last = V.tensor_copy(xraw[:, m, :, 1:S + 1], bank(4 + m, 2, S))
            done(last, "kraw")
            done(conv(halves(kc), 4, 2), "kc_conv")
            for m in range(4):
                ve.wait_ge(*at("v2_proj", m + 1))
                last = V.tensor_copy(xraw[:, m, :, 1:S + 1], bank(m, 2, S))
            done(last, "vraw")
            done(conv(halves(vc), 8, 2), "vc_conv")
            ve.wait_ge(*at("q_proj", 1))
            V.tensor_copy(xraw[:, 0:2, 0, 1:S + 1], bank(4, 2, S))
            done(V.tensor_copy(xraw[:, 2:4, 0, 1:S + 1], bank(5, 2, S)), "qraw")
            done(conv(lambda m: qc[:, m:m + 1, :], 0, 1), "qc_conv")
            ve.wait_ge(*at("ba_proj", 1))
            ve.wait_ge(*at("dt_in", 32))
            ba = ps[:, 6, 0:64].rearrange("p (t n) -> p t n", t=4)
            done(V.tensor_tensor(gdec, ba[:, :, 8:16], rep(dtb, 4), ALU.add), "g_pre")
            ve.wait_ge(*at("sp_ln", 1))
            done(V.tensor_scalar(gdec, gdec, 0.0, None, ALU.max))
            done(V.tensor_tensor(gdec, gdec, spa, ALU.add))
            done(V.scalar_tensor_tensor(gdec, gdec, -1.0, rep(alog, 4), ALU.mult, ALU.mult), "gdec_ready")
            ve.wait_ge(*at("gcs_sum", 1))
            done(V.tensor_copy(gcs, ps[:, 7, 0:32].rearrange("p (t n) -> p t n", t=4)), "gcs_ready")
            ve.wait_ge(*at("egc_ready", 1))
            done(V.tensor_tensor(bg, beta, egc, ALU.mult), "bg_ready")
            ve.wait_ge(*at("k_rs", 1))
            done(V.tensor_tensor(kF, kc, sq, ALU.mult), "kF_ready")
            ve.wait_ge(*at("vT_ready", 1))
            for t in range(4):
                last = V.tensor_copy(vTok[:, t, :, :], bank(4 + t, 4, P))
            done(last, "vTok_ready")
            ve.wait_ge(*at("q_rs", 1))
            done(V.scalar_tensor_tensor(qF, qc, P ** -0.5, sq[:, :, 0:S], ALU.mult, ALU.mult), "qF_ready")
            for s_ in range(4):
                x_part = s_ >= 2
                for d in range(2):
                    n, b, t = 2 * s_ + d, 4 * d, TILE[d][s_]
                    A, dl, D_, DT, eR = WK[d][0], WK[d][1], WK[d][6], WK[d][8], WK[d][7]
                    last_tok = (P - 1, 0)[d]
                    gc4 = gcs[:, t, 4 * d:4 * d + 4]
                    ve.wait_ge(*at("gram", n + 1))
                    R = bank(b + 1, 4, P)
                    V.tensor_tensor(kdl[d], R[:, :, last_tok], gc4, ALU.subtract)
                    done(V.tensor_tensor(dl, R, over(gc4, P), ALU.subtract))
                    if x_part:
                        V.tensor_scalar(DT, dl, 0.0, None, ALU.min)
                    done(V.tensor_scalar(D_, dl, 0.0, None, ALU.max), "D_pre")
                for d in range(2):
                    n, b, t = 2 * s_ + d, 4 * d, TILE[d][s_]
                    A, D_, DT = WK[d][0], WK[d][6], WK[d][8]
                    ve.wait_ge(*at("D_exp", n + 1))
                    for h in range(H):
                        last = V.scalar_tensor_tensor(A[:, h, :], ps[:, b, h * P:(h + 1) * P], beta[:, t, 4 * d + h:4 * d + h + 1],
                                                      D_[:, h, :], ALU.mult, ALU.mult)
                    done(last, "A_ready")
                    if x_part:
                        done(V.tensor_tensor(DT, DT, bank(b + 2, 4, P), ALU.mult))
                        done(V.tensor_tensor(DT, DT, rep((tri_le, tri_ge)[d], 4), ALU.mult), "attT_dn")
                    T, tmp = WK[d][4], WK[d][6]
                    done(V.tensor_tensor(tmp, A, rep(level_mask(0, d == 1), 4), ALU.mult))
                    done(V.tensor_tensor(T, rep(ident, 4), tmp, ALU.subtract))
                for d in range(2):
                    At, U, tmp = WK[d][1], WK[d][5], WK[d][6]
                    ve.wait_ge(*at("At_copied", 2 * s_ + d + 1))
                    done(V.tensor_tensor(tmp, At, rep(level_mask(0, d == 0), 4), ALU.mult))
                    done(V.tensor_tensor(U, rep(ident, 4), tmp, ALU.subtract), "TU_ready")
                for l in range(1, len(LEVELS)):
                    for d in range(2):
                        T, U = WK[d][4], WK[d][5]
                        ve.wait_ge(*at("TU_step", p1_count(s_, d, l)))
                        if l < len(LEVELS) - 1:
                            V.tensor_tensor(T, T, bank(4 * d + 2, 4, P), ALU.subtract)
                        done(V.tensor_tensor(U, U, bank(4 * d + 3, 4, P), ALU.subtract), "TU_ready")
                for d in range(2):
                    ve.wait_ge(*at("vnew", 2 * s_ + d + 1))
                    done(V.tensor_copy(WK[d][4], bank(4 * d + 2, 4, P)), "vn_ready")
                for d in range(2):
                    n, b, t = 2 * s_ + d, 4 * d, TILE[d][s_]
                    ve.wait_ge(*at("dS_ready", n + 1))
                    if x_part:
                        o_ = oF[:, :, t * P:(t + 1) * P]
                        if s_ == 2:
                            V.tensor_copy(o_, bank(b + 3, 4, P))
                        else:
                            V.tensor_tensor(o_, o_, bank(b + 3, 4, P), ALU.add)
                    if s_ == 0:
                        done(V.tensor_copy(Sd[d], bank(b, 4, P)), "S_ready")
                    else:
                        ve.wait_ge(*at("eR", n + 1))
                        done(V.tensor_tensor(Sd[d], Sd[d], over(egl[d], P), ALU.mult))
                        done(V.tensor_tensor(Sd[d], Sd[d], bank(b, 4, P), ALU.add), "S_ready")

            def gated(i, o_, g_, dst, src_of):
                ve.wait_ge(*at("rs_done", i + 1))
                done(V.scalar_tensor_tensor(rs, rs, g_, o_, ALU.mult, ALU.mult))
                ve.wait_ge(*at("z_silu", i + 1))
                done(V.tensor_tensor(dst, src_of(rs), src_of(zs), ALU.mult), "y_gated")

            gated(0, oF, colB("dn_norm_g_2"), oF, lambda v: v)
            done(V.tensor_tensor(lbl, colB("hg_lb_logits_2", 0, 4), colB("hg_lb_logits_2", 0, 4), ALU.subtract), "lb_shift")
            ve.wait_ge(*at("lb_exp", 1))
            done(V.reciprocal(lbw, lbe))
            done(V.tensor_tensor(lbw, lbw, lbe, ALU.mult))
            done(V.tensor_tensor(lb, lbw, lbw, ALU.subtract))
            done(V.tensor_scalar(omlb, lb, -1.0, 1.0, ALU.mult, ALU.add))
            for d in range(2):
                ve.wait_ge(*at("f_sig", d + 1))
                for h in range(H):
                    V.tensor_scalar(ff[:, h, :], ff[:, h, :], omlb[:, h:h + 1], lb[:, h:h + 1], ALU.mult, ALU.add)
                    last = V.tensor_scalar(kk[:, h, :], kk[:, h, :], omlb[:, h:h + 1], None, ALU.mult)
                done(last, "kk_ready")
                done(V.tensor_scalar(ff, ff, LN_TINY, None, ALU.max))
                done(V.tensor_scalar(f2, ff, 2.0 ** 60, 1.0, ALU.mult, ALU.min))
                done(V.tensor_scalar(ff, ff, 2.0 ** -60, None, ALU.max), "f_parts")
                ve.wait_ge(*at("f_ln", d + 1))
                done(V.tensor_tensor(ff, ff, f2, ALU.add))
                step = 1 if d == 0 else -1
                for h in range(H):
                    for q_ in range(2):
                        o_ = gg[:, h, q_ * S:(q_ + 1) * S][:, ::step]
                        i_ = ff[:, h, q_ * S:(q_ + 1) * S][:, ::step]
                        last = V.tensor_tensor_scan(o_, ones[:, 0:1].to_broadcast([P, S]), i_, 0.0, ALU.mult, ALU.add)
                done(last, "gg_ready")
                ve.wait_ge(*at("kd_exp", d + 1))
                done(V.tensor_tensor(Wd, Wd, kk[:, :, S:2 * S], ALU.mult), "kd_ready")
                if d == 0:
                    ve.wait_ge(*at("hi_proj", 1))
                    for t in range(4):
                        last = V.tensor_copy(hv[:, t, :], ps[:, t, :])
                    done(last, "hv_ready")
                    done(V.memset(qW, 0.0))
                    done(V.memset(kW, 0.0))
                ve.wait_ge(*at("eg_exp", d + 1))
                done(V.tensor_tensor(qe, hq, eg, ALU.mult), "qe_ready")
                ve.wait_ge(*at("Sg_sum", d + 1))
                done(V.tensor_copy(Sg, bank(2, 4, P)), "Sg_ready")

                def mask(l):
                    n = 8 * d + l
                    ve.wait_ge(*at("att_ready", n + 1))
                    m_ = ident if l == 0 else level_mask(l - 1, d == 0)
                    dst = attT if l == 0 else atmp
                    if l >= 2:
                        ve.wait_ge(*at("att_sum", n))
                    for t in range(NT):
                        last = V.tensor_tensor(dst[:, t, :, :], bank(4 + 2 * (l % 2) + t, 4, P), rep(m_, 4), ALU.mult)
                    done(last, "att_masked")

                for l in range(8):
                    b = 1 << l
                    qs = 1 - d
                    ve.wait_ge(*at("W_exp", 8 * d + l + 1))
                    ve.wait_ge(*at("att_ready", 8 * d + l + 1))

                    def half(v, side):
                        return v.rearrange("p h (n s b) -> p (h n) s b", s=2, b=b)[:, :, side, :]

                    def half_k(side):
                        return kk[:, :, 0:S].rearrange("p h (n s b) -> p h n s b", s=2, b=b)[:, :, :, side, :]

                    V.tensor_tensor(half(qW, qs), half(hq, qs), half(Wx, qs), ALU.mult)
                    kw_h = kW.rearrange("p h (n s b) -> p h n s b", s=2, b=b)[:, :, :, 1 - qs, :]
                    wx_h = Wx.rearrange("p h (n s b) -> p h n s b", s=2, b=b)[:, :, :, 1 - qs, :]
                    done(V.tensor_tensor(kw_h, half_k(1 - qs), wx_h, ALU.mult), "W_ready")
                    mask(l)
                ve.wait_ge(*at("attX_sum", d + 1))
                done(V.tensor_copy(attX, bank(3, 4, P)), "attX_ready")
                ve.wait_ge(*at("og_sum", d + 1))
                for t in range(NT):
                    o_ = og[:, :, t * P:(t + 1) * P]
                    if d == 0:
                        last = V.tensor_copy(o_, bank(t, 4, P))
                    else:
                        last = V.tensor_tensor(o_, o_, bank(t, 4, P), ALU.add)
                done(last, "og_ready")
            ve.wait_ge(*at("rs_done", 2))
            done(V.scalar_tensor_tensor(rs, rs, colB("hg_norm_g_2"), og, ALU.mult, ALU.mult))
            ve.wait_ge(*at("z_silu", 2))
            for h in range(H):
                last = V.tensor_tensor(permuted(yhg[:, h, :]), rs[:, h, :].rearrange("p (c r) -> p c r", r=4),
                                       zh[:, h, :].rearrange("p (c r) -> p c r", r=4), ALU.mult)
            done(last, "y_gated")
            for c in range(8):
                last = V.tensor_scalar(dg[:, c, :], ident, mod[:, 16 + c, 0:1], None, ALU.mult)
            done(last, "dg_ready")
            ve.wait_ge(*at("gate_sig", 4))
            for c in range(4):
                ve.wait_ge(*at("br", c + 1))
                gate = gd0[:, 2 * c:2 * c + 2, :] if c < 2 else sgt[:, 2 * c:2 * c + 2, :]
                done(V.tensor_tensor(mg[:, 2 * c:2 * c + 2, :], bank(4 + c, 2, S), gate, ALU.mult), "br_read")
            for c in range(4):
                ve.wait_ge(*at("br", 4 + c + 1))
                done(V.tensor_tensor(mtmp, bank(4 + c, 2, S), sgt[:, 8 + 2 * c:10 + 2 * c, :], ALU.mult))
                done(V.tensor_tensor(mg[:, 2 * c:2 * c + 2, :], mg[:, 2 * c:2 * c + 2, :], mtmp, ALU.add), "mg_ready" if c == 3 else "ve_step")
            ve.wait_ge(*at("grow_ready", 1))
            for n in range(2):
                ve.wait_ge(*at("y2_ready", n + 1))
                for t in range(NT):
                    done(V.tensor_tensor(sgt[:, 2 * (2 * n + t):2 * (2 * n + t) + 2, :], bank(4 + 2 * n + t, 2, S),
                                         grow[:, n * 512:(n + 1) * 512].rearrange("p (a b) -> p a b", a=2), ALU.mult))
                    last = V.tensor_tensor(res[:, t, n * 512:(n + 1) * 512], res[:, t, n * 512:(n + 1) * 512],
                                           sgt[:, 2 * (2 * n + t):2 * (2 * n + t) + 2, :].rearrange("p a b -> p (a b)"), ALU.add)
            for c in range(8):
                last2 = V.tensor_scalar(dg2[:, c, :], ident, mod[:, 40 + c, 0:1], None, ALU.mult)
            done(last2, "dg_ready")
            done(V.memset(lams[:, 7:8], 0.0), "res_ready")
            norm(7)
            norm_modulate(hTx, gM, mod[:, 24:32, 0], "hT_ready")
            ve.wait_ge(*at("logits_ready", 2))
            done(V.tensor_tensor(lg36, ps[:, 6, 0:NT * 36].rearrange("p (t e) -> p t e", t=NT), rep(brt, NT), ALU.add))
            grp = lg36[:, :, 0:4]
            goh, gdf = oh1[:, :, 0:4], oh2[:, :, 0:4]
            top(4, grp, gmx, goh)
            done(V.tensor_tensor(gdf, grp, over(gmx, 4), ALU.subtract), "grp_shift")
            ve.wait_ge(*at("grp_exp", 1))
            done(V.tensor_reduce(gsum, gdf, AX.X, ALU.add))
            done(V.reciprocal(gprob, gsum))
            done(V.tensor_scalar(goh, goh, BIG, -BIG, ALU.mult, ALU.add))
            for t in range(NT):
                last = V.tensor_tensor(lgt[:, t, :].rearrange("p (g e) -> p g e", g=4), lg36[:, t, 4:36].rearrange("p (g e) -> p g e", g=4),
                                       over(goh[:, t, :], 8), ALU.add)
            done(last)
            route(moe2, lgt, gprob)
            done(V.memset(facc, 0.0))

            def copy2(x_):
                C = moe2.W
                for b in range(2):
                    x4 = x_[:, 4 * b:4 * b + 4, :]
                    for k in range(4):
                        c = 4 * b + k
                        last = V.tensor_scalar(x_[:, c, :], ps[:, 2 + b, k * C:(k + 1) * C], gM[:, c:c + 1],
                                               mod[:, 24 + c, 0:1], ALU.mult, ALU.add)
                return last

            routed(moe2, facc, copy2)
            done(V.tensor_tensor(facc, facc, frow[:, None, :].to_broadcast([P, NT, D]), ALU.mult))
            done(V.tensor_tensor(res[:, :, :], res[:, :, :], facc, ALU.add), "res_ready")
            norm(8)
            ve.wait_ge(*at("glrow_in", 16))
            for t in range(NT):
                last = V.tensor_tensor(res[:, t, :], xn[:, t, :], glrow, ALU.mult)
            done(last, "result")

        @block.scalar
        def _(ac):
            def act(*a, **k):
                return nc.scalar.activation(*a, **k)

            def done(ins_, name="ac_step"):
                count[name] = count.get(name, 0) + 1
                ins_.then_inc(inc(name), 1)
                ac.wait_ge(*at(name, count[name]))

            def norm(i, src=res, need=None):
                name, value = need or ("res_ready", i)
                ac.wait_ge(*at(name, value))
                for t in range(NT):
                    last = act(xn[:, t, :], src[:, t, :], ACT.Square, accum_out=ss[:, t:t + 1])
                done(last, "sumsq")
                ac.wait_ge(*at("ms_ready", i + 1))
                done(act(lnv, ms, ACT.Ln))
                done(act(rstd, lnv, ACT.Exp, scale=-0.5), "rstd_ready")

            def route(moe):
                ac.wait_ge(*at("top%d_diff" % moe.n, 1))
                done(act(e2_, dm, ACT.Exp), "top%d_exp" % moe.n)
                ac.wait_ge(*at("rounds%d_ready" % moe.n, 1))

            def moe_round(moe, x, R):
                C, U, E = moe.W, moe.U, moe.E
                N = moe.chunks
                nm = "m%d_" % moe.n

                def silu(n, c):
                    i, own = c % (4 * moe.per), moe.own(c)
                    ac.wait_ge(*at(nm + "gu", n + 1))
                    ac.wait_ge(*at(nm + "act", n + 1))
                    act(m_sg[:, i, own], ps[:, i % 2, own], ACT.Silu).then_inc(inc(nm + "sg"), 1)

                def turned(g, b):
                    ac.wait_ge(*at(nm + "gath", R * (E + 1) + g + 1))
                    act(GcT[0:C, b, :, :], ps[0:C, 6, 0:NT * P].rearrange("p (t q) -> p t q", t=NT), ACT.Copy).then_inc(inc(nm + "gcT"), 1)

                turned(0, 0)
                with ac.Fori(0, E // 2) as p:
                    for b in range(2):
                        e = 2 * p + b
                        n0 = R * N + 4 * U * e
                        if moe.per == 1:
                            with ac.Fori(0, U) as j:
                                for i in range(4):
                                    silu(n0 + 4 * j + i, i)
                        else:
                            for c in range(4 * U):
                                silu(n0 + c, c)
                        turned(e + 1, 1 - b)
                        ac.wait_ge(*at(nm + "dn", n0 + 4 * U + 4))
                        act(ysb[0:C, 0:512], ps[0:C, 4, :], ACT.Copy)
                        act(ysb[0:C, 512:D], ps[0:C, 5, :], ACT.Copy).then_inc(inc(nm + "y"), 1)

            def routed(moe):
                moe_round(moe, "m", 0)
                rounds = ac.value_load(rounds_i[moe.n - 1][0:1, 0:1], min_val=1, max_val=8)
                with ac.If(rounds > 1):
                    with ac.Fori(1, rounds) as r:
                        moe_round(moe, "x", r)

            ac.dma_start(rowsA[OFF_A["ln_mix_even"][0]:8, :], ins["ln_mix_even"][0].rearrange("(r d) -> r d", d=P)).then_inc(inc("rows_in"), 16)
            for name, n in ROWS_A[1:]:
                o = OFF_A[name][0]
                v = ins[name][0]
                if len(v.shape) == 2:
                    v = v.rearrange("a b -> (a b)")
                ac.dma_start(rowsA[o:o + n, :], v.rearrange("(r d) -> r d", d=P)).then_inc(inc("rows_in"), 16)
            for name, n in ROWS_B:
                o = OFF_B[name][0]
                v = ins[name] if name == "c_ctx_2" else ins[name][0]
                if len(v.shape) == 2:
                    v = v.rearrange("a b -> (a b)")
                ac.dma_start(rowsB[o:o + n, :], v.rearrange("(r d) -> r d", d=P)).then_inc(inc("rows_in"), 16)
            ac.wait_ge(*at("cols_ready", 1))
            ac.wait_ge(*at("lam_dot", 1))
            done(act(lams[:, 2:4], lams[:, 0:2], ACT.Exp), "lam_exp")
            done(act(nl, colA("rg_lam", 0, 4), ACT.Abs))
            done(act(nl2, nl, ACT.Exp, scale=-1.0))
            done(act(nl2, nl2, ACT.Ln, bias=1.0), "nl_ln")
            act(scT[:, :, 0], colB("c_2", 0, 8), ACT.Silu)
            done(act(scT[:, :, 1], colB("c_ctx_2", 0, 8), ACT.Silu), "c_silu")
            norm(0, res, ("x_in", 16))
            ac.wait_ge(*at("gb_proj", 1))
            act(gbF[:, 0:2, :], bank(4, 2, S), ACT.Copy)
            done(act(gbF[:, 2:4, :], bank(5, 2, S), ACT.Copy), "gb_copied")

            def mod_rows(i0, i1):
                for i in range(i0, i1):
                    ac.wait_ge(*at("ada", i + 1))
                    if i >= 2:
                        ac.wait_ge(*at("ada_cols", i - 1))
                    act(modrow[0:2, i % 2, :], ps[0:2, 5 + i % 2, :], ACT.Copy).then_inc(inc("mod_row"), 1)

            ac.wait_ge(*at("hT_ready", 1))
            for qt in range(NT):
                nk = P * (qt + 1)
                ac.wait_ge(*at("s_shifted", qt + 1))
                done(act(sc[:, :, 0:nk], sc[:, :, 0:nk], ACT.Exp, scale=0.125), "s_exp")
                mod_rows(6 * qt, 6 * qt + 4)
                ac.wait_ge(*at("o_ms", qt + 1))
                done(act(o4c, o4b, ACT.Ln))
                done(act(o4c, o4c, ACT.Exp, scale=-0.5), "o_rstd")
                mod_rows(6 * qt + 4, 6 * qt + 6)
            ac.wait_ge(*at("gelu_in", 1))
            done(act(gel, gt, ACT.Tanh, scale=0.7978845608028654), "gelu_tanh")
            ac.wait_ge(*at("gates_ready", 1))
            for m in range(4):
                act(rg_r[:, m, :], ps[:, m // 2, (m % 2) * S:(m % 2 + 1) * S], ACT.Sigmoid, bias=colA("rg_ba", m))
                last = act(rg_i[:, m, :], ps[:, 2 + m // 2, (m % 2) * S:(m % 2 + 1) * S], ACT.Sigmoid, bias=colA("rg_bx", m))
            done(last, "rg_sig")
            ac.wait_ge(*at("log_a", 1))
            done(act(rg_a, rg_r, ACT.Exp))
            done(act(rg_r, rg_r, ACT.Tanh), "rg_exp")
            ac.wait_ge(*at("one_minus", 1))
            done(act(rg_u, rg_u, ACT.Sqrt), "rg_sqrt")
            norm(1)
            for n in range(FFN // P):
                ac.wait_ge(*at("gu_ready", n + 1))
                if n >= 4:
                    ac.wait_ge(*at("act_ready", n - 3))
                act(sgb[:, n % 4, :], ps[:, n % 4, 0:256], ACT.Silu).then_inc(inc("sg_ready"), 1)
            norm(2)
            ac.wait_ge(*at("ctx_in", 16))
            norm(3, cres, ("poolT_copied", 1))
            ac.wait_ge(*at("hTc_ready", 1))
            norm(4, res, ("res_ready", 3))
            route(moe1)
            routed(moe1)
            norm(5, res, ("res_ready", 4))
            norm(6, res, ("res_ready", 5))
            ac.wait_ge(*at("kc_conv", 1))
            done(act(kc, kc, ACT.Silu))
            done(act(sq, kc, ACT.Square), "k_sq")
            ac.wait_ge(*at("vc_conv", 1))
            done(act(vc, vc, ACT.Silu), "vc_ready")
            ac.wait_ge(*at("qc_conv", 1))
            done(act(qc, qc, ACT.Silu))
            ba = ps[:, 6, 0:64].rearrange("p (t n) -> p t n", t=4)
            ac.wait_ge(*at("g_pre", 1))
            done(act(beta, ba[:, :, 0:8], ACT.Sigmoid), "ba_read")
            done(act(alog, alog, ACT.Exp))
            done(act(spa, gdec, ACT.Abs))
            done(act(spa, spa, ACT.Exp, scale=-1.0))
            done(act(spa, spa, ACT.Ln, bias=1.0), "sp_ln")
            ac.wait_ge(*at("k_ss", 1))
            done(act(sq, ps[:, 0:4, :], ACT.Ln, bias=epsc))
            done(act(sq, sq, ACT.Exp, scale=-0.5), "k_rs")
            ac.wait_ge(*at("gcs_ready", 1))
            done(act(egc, gcs, ACT.Exp), "egc_ready")
            ac.wait_ge(*at("kT_ready", 1))
            done(act(kTok, ps[:, 0:4, :].rearrange("p t (h q) -> p t h q", h=H), ACT.Copy), "kTok_ready")
            done(act(sq[:, :, 0:S], qc, ACT.Square), "q_sq")
            ac.wait_ge(*at("q_ss", 1))
            done(act(sq[:, :, 0:S], ps[:, 0:2, :].rearrange("p b (h q) -> p (b h) q", h=2), ACT.Ln, bias=epsc))
            done(act(sq[:, :, 0:S], sq[:, :, 0:S], ACT.Exp, scale=-0.5), "q_rs")
            for s_ in range(4):
                x_part = s_ >= 2
                for d in range(2):
                    n, b = 2 * s_ + d, 4 * d
                    D_, DT, eR = WK[d][6], WK[d][8], WK[d][7]
                    last_tok = (P - 1, 0)[d]
                    ac.wait_ge(*at("D_pre", n + 1))
                    act(D_, D_, ACT.Exp, scale=-1.0)
                    if x_part:
                        act(DT, DT, ACT.Exp)
                    done(act(kdl[d], kdl[d], ACT.Exp), "D_exp")
                    act(egl[d], bank(b + 1, 4, P)[:, :, last_tok], ACT.Exp)
                    done(act(eR, bank(b + 1, 4, P), ACT.Exp), "eR")
                for d in range(2):
                    ac.wait_ge(*at("At_ready", 2 * s_ + d + 1))
                    done(act(WK[d][1], bank(4 * d, 4, P), ACT.Copy), "At_copied")
                for l in range(1, len(LEVELS)):
                    for d in range(2):
                        ac.wait_ge(*at("P1_ready", p1_count(s_, d, l)))
                        done(act(WK[d][6], bank(4 * d + 1, 4, P), ACT.Copy), "P1_copied")
                for d in range(2):
                    ac.wait_ge(*at("wT_dn", 2 * s_ + d + 1))
                    done(act(WK[d][2], bank(4 * d + 1, 4, P), ACT.Copy, scale=-1.0), "nw_ready")

            ac.wait_ge(*at("S_ready", 8))
            done(act(rs, oF, ACT.Square), "o_sq")
            ac.wait_ge(*at("zd_proj", 1))
            done(act(zs, ps[:, 0:2, :].rearrange("p b (h q) -> p (b h) q", h=2), ACT.Silu), "z_silu")
            ac.wait_ge(*at("o_ss", 1))
            done(act(rs, ps[:, 2:4, :].rearrange("p b (h q) -> p (b h) q", h=2), ACT.Ln, scale=1.0 / P, bias=epsc))
            done(act(rs, rs, ACT.Exp, scale=-0.5), "rs_done")
            ac.wait_ge(*at("lb_shift", 1))
            done(act(lbe, lbl, ACT.Exp), "lb_exp")
            ac.wait_ge(*at("hq_proj", 1))
            ac.wait_ge(*at("y_gated", 1))
            for h in range(H):
                last = act(hq[:, h, :].rearrange("p (c r) -> p c r", r=4), permuted(ps[:, 4 + h // 2, (h % 2) * S:(h % 2 + 1) * S]), ACT.Silu)
            done(last, "hq_ready")
            for d in range(2):
                ac.wait_ge(*at("f_proj", d + 1))
                if d == 1:
                    ac.wait_ge(*at("og_sum", 1))
                for h in range(H):
                    for dst, sign in ((ff, 1.0), (kk, -1.0)):
                        act(dst[:, h, 0:S].rearrange("p (c r) -> p c r", r=4), permuted(ps[:, 4 + h, 0:S]), ACT.Sigmoid, scale=sign)
                        last = act(dst[:, h, S:2 * S], ps[:, 4 + h, S:2 * S], ACT.Sigmoid, scale=sign)
                done(last, "f_sig")
                ac.wait_ge(*at("f_parts", d + 1))
                act(f2, f2, ACT.Ln)
                done(act(ff, ff, ACT.Ln), "f_ln")
                ac.wait_ge(*at("gg_ready", d + 1))
                end = 2 * S - 1 if d == 0 else S
                for h in range(H):
                    last = act(Wd[:, h, :], gg[:, h, S:2 * S], ACT.Exp, scale=-1.0, bias=gg[:, h, end:end + 1])
                done(last, "kd_exp")
                done(act(eg, gg[:, :, 0:S], ACT.Exp), "eg_exp")
                if d == 1:
                    ac.wait_ge(*at("hz_proj", 1))
                    for h in range(H):
                        last = act(zh[:, h, :].rearrange("p (c r) -> p c r", r=4), permuted(ps[:, 4 + h // 2, (h % 2) * S:(h % 2 + 1) * S]), ACT.Silu)
                    done(last, "z_silu")
                    ac.wait_ge(*at("gate_proj", 1))
                    done(act(gd0, ps[:, 6:8, :].rearrange("p b (h q) -> p (b h) q", h=2), ACT.Sigmoid), "gate_sig")
                ac.wait_ge(*at("kdT_ready", d + 1))
                done(act(kdTok, ps[:, 0:2, :].rearrange("p t (h q) -> p t h q", h=H), ACT.Copy), "kdTok_ready")
                for l in range(8):
                    ac.wait_ge(*at("Wd_ready", 8 * d + l + 1))
                    if l >= 1:
                        ac.wait_ge(*at("W_ready", 8 * d + l))
                    done(act(Wx, Wd, ACT.Exp), "W_exp")
            ac.wait_ge(*at("og_ready", 2))
            done(act(rs, og, ACT.Square), "o_sq")
            ac.wait_ge(*at("o_ss", 2))
            done(act(rs, ps[:, 6:8, :].rearrange("p b (h q) -> p (b h) q", h=2), ACT.Ln, scale=1.0 / P, bias=epsc))
            done(act(rs, rs, ACT.Exp, scale=-0.5), "rs_done")
            ac.wait_ge(*at("y_gated", 2))
            for i in range(1, 4):
                ac.wait_ge(*at("gate_proj", i + 1))
                done(act(sgt[:, 4 * i:4 * i + 4, :], ps[:, 2 * (i % 2):2 * (i % 2) + 2, :].rearrange("p b (h q) -> p (b h) q", h=2),
                         ACT.Sigmoid), "gate_sig")
            ac.wait_ge(*at("grow_sum", 1))
            done(act(grow.rearrange("p (a b) -> p a b", a=2), ps[:, 0:2, :], ACT.Copy), "grow_ready")
            norm(7, res, ("res_ready", 6))
            ac.wait_ge(*at("grow_sum", 2))
            done(act(frow.rearrange("p (a b) -> p a b", a=2), ps[:, 4:6, :], ACT.Copy), "frow_ready")
            gdf = oh2[:, :, 0:4]
            ac.wait_ge(*at("grp_shift", 1))
            done(act(gdf, gdf, ACT.Exp), "grp_exp")
            route(moe2)
            routed(moe2)
            norm(8, res, ("res_ready", 7))

        @block.gpsimd
        def _(po):
            G = nc.gpsimd
            po.dma_start(res[:, :, :], ins["x"][0].rearrange("(t p) d -> p t d", p=P)).then_inc(inc("x_in"), 16)
            po.dma_start(table[:, :], ins["k_table"]).then_inc(inc("table_in"), 16)
            po.dma_start(const1, ins["k_table1"]).then_inc(inc("table1_in"), 16)
            for i, name in enumerate(("lam_q1", "lam_q2", "lam_k1", "lam_k2")):
                po.dma_start(lamv[:, i, :], ins[name].to_broadcast([P, 64])).then_inc(inc("lam_in"), 16)
            po.wait_ge(*at("hT_ready", 1))
            G.memset(wgate, 0.0).then_inc(inc("wgate_zero"), 1)
            po.wait_ge(*at("wgate_zero", 1))
            for g, name in enumerate(("rg_wa", "rg_wx")):
                for h in range(8):
                    o = 64 * (h % 2)
                    po.dma_start(wgate[o:o + 64, g, h // 2, o:o + 64], ins[name][0, h]).then_inc(inc("wgate_in"), 16)
            po.wait_ge(*at("act_ready", 1))
            po.dma_start(cres, ins["ctx_2"][0].rearrange("(t p) d -> p t d", p=P)).then_inc(inc("ctx_in"), 16)
            po.dma_start(rw1, ins["router_w"][0].rearrange("(k p) e -> p k e", p=P)).then_inc(inc("router1_in"), 16)
            po.dma_start(brow, ins["pool_scale"].to_broadcast([P, D])).then_inc(inc("pool_scale_in"), 16)
            po.dma_start(fgrow, ins["final_g"][None, :].to_broadcast([P, D])).then_inc(inc("fgrow_in"), 16)
            po.dma_start(wba[:, :, :], ins["w_in_2"][0, :, 2048:2064].rearrange("(k p) n -> p k n", p=P)).then_inc(inc("wba_in"), 16)
            po.dma_start(alog, ins["dn_a_log_2"][0].rearrange("a b -> (a b)")[None, :].to_broadcast([P, 8])).then_inc(inc("dt_in"), 16)
            po.dma_start(dtb, ins["dn_dt_bias_2"][0].rearrange("a b -> (a b)")[None, :].to_broadcast([P, 8])).then_inc(inc("dt_in"), 16)
            po.wait_ge(*at("bg_ready", 1))
            po.wait_ge(*at("vTok_ready", 1))
            po.wait_ge(*at("kTok_ready", 1))
            po.wait_ge(*at("qF_ready", 1))
            for s_ in range(4):
                for l in range(1, len(LEVELS)):
                    for d in range(2):
                        if l == 1:
                            po.wait_ge(*at("At_copied", 2 * s_ + d + 1))
                        if l >= 3:
                            po.wait_ge(*at("P1_ready", p1_count(s_, d, l - 2)))
                        G.tensor_tensor(WK[d][2 + l % 2], WK[d][1], rep(level_mask(l, d == 0), 4), ALU.mult)\
                            .then_inc(inc("Aoff_ready"), 1)
                for d in range(2):
                    n, t = 2 * s_ + d, TILE[d][s_]
                    po.wait_ge(*at("TU_step", p1_count(s_, d, 6)))
                    G.tensor_tensor(WK[d][3], vTok[:, t, :, :], over(beta[:, t, 4 * d:4 * d + 4], P), ALU.mult)
                    po.wait_ge(*at("Aoff_ready", 12 * s_ + 12))
                    G.tensor_tensor(WK[d][1], kTok[:, t, :, :], over(kdl[d], P), ALU.mult)
                    if s_ >= 2:
                        po.wait_ge(*at("eR", n + 1))
                        G.tensor_tensor(WK[d][7], qF[:, :, t * P:(t + 1) * P], WK[d][7], ALU.mult)
                    G.tensor_tensor(WK[d][6], kTok[:, t, :, :], over(bg[:, t, 4 * d:4 * d + 4], P), ALU.mult).then_inc(inc("kbg_ready"), 1)
                    po.wait_ge(*at("kbg_ready", n + 1))
            po.wait_ge(*at("S_ready", 8))
            for k in range(KC):
                last = G.tensor_copy(hxp[:, k, :].rearrange("p (c r) -> p c r", r=4), permuted(hT[:, k, 0:S]))
            last.then_inc(inc("hxp_ready"), 1)
            for d in range(2):
                def add(l):
                    n = 8 * d + l
                    po.wait_ge(*at("att_masked", n + 1))
                    if l == 0:
                        po.sem_inc(sem("att_sum"), 1)
                    else:
                        G.tensor_tensor(attT, attT, atmp, ALU.add).then_inc(inc("att_sum"), 1)
                        po.wait_ge(*at("att_sum", n + 1))

                for l in range(8):
                    b = 1 << l
                    qs, nb = 1 - d, S // (2 * b)
                    if l == 0:
                        po.wait_ge(*at("gg_ready", d + 1))
                        po.wait_ge(*at("Sg_sum", d + 1))
                    else:
                        po.wait_ge(*at("W_exp", 8 * d + l))
                    for h in range(H):
                        g_h = gg[:, h, 0:S].rearrange("p (n s b) -> p n s b", s=2, b=b)
                        mid = (g_h[:, :, 0, b - 1:b] if d == 0 else g_h[:, :, 1, 0:1]).to_broadcast([P, nb, b])
                        w_h = Wd[:, h, :].rearrange("p (n s b) -> p n s b", s=2, b=b)
                        G.tensor_tensor(w_h[:, :, qs, :], g_h[:, :, qs, :], mid, ALU.subtract)
                        last = G.tensor_tensor(w_h[:, :, 1 - qs, :], mid, g_h[:, :, 1 - qs, :], ALU.subtract)
                    last.then_inc(inc("Wd_ready"), 1)
                    if l:
                        add(l - 1)
                add(7)
            po.wait_ge(*at("res_ready", 6))
            with nc.allow_non_contiguous_dma(reason="router columns"):
                po.dma_start(wre[:, :, 0:4], ins["w_router_grp_2"][0].rearrange("(k p) n -> p k n", p=P)).then_inc(inc("router2_in"), 16)
                po.dma_start(wre[:, :, 4:36], ins["w_router_exp_2"][0].rearrange("(k p) n -> p k n", p=P)).then_inc(inc("router2_in"), 16)
            po.dma_start(brt[:, 0:4], ins["b_router_grp_2"].to_broadcast([P, 4])).then_inc(inc("router2_in"), 16)
            po.dma_start(brt[:, 4:36], ins["b_router_exp_2"].to_broadcast([P, 32])).then_inc(inc("router2_in"), 16)
            po.dma_start(glrow, ins["g_final_2"][None, :].to_broadcast([P, D])).then_inc(inc("glrow_in"), 16)


NAMES = ["x", "ln_mix_even", "w_in_even", "lam_q1", "lam_k1", "lam_q2", "lam_k2", "subln_g", "conv_w", "conv_b",
         "rg_wa", "rg_ba", "rg_wx", "rg_bx", "rg_lam", "w_out_even", "ln_ffn_even", "ffn_wg", "ffn_wu", "ffn_wd",
         "ln_mix_odd", "pool_w", "pool_scale", "ln_ffn_odd", "router_w", "moe_wg", "moe_wu", "moe_wd", "final_g",
         "c_2", "ctx_2", "c_ctx_2", "w_ada_2", "b_ada_2", "g_mix_2", "g_ffn_2", "g_final_2", "w_in_2", "dn_conv_2",
         "dn_a_log_2", "dn_dt_bias_2", "dn_norm_g_2", "hg_lb_logits_2", "hg_norm_g_2", "w_br_dn_2", "w_br_hg_2",
         "w_out_2", "w_router_grp_2", "b_router_grp_2", "w_router_exp_2", "b_router_exp_2", "w_exp_gate_2",
         "w_exp_up_2", "w_exp_down_2"]


def kernel(**inputs):
    import concourse.bacc as bacc
    from concourse.bass_utils import run_bass_kernel_spmd

    nc = bacc.Bacc("TRN2", target_bir_lowering=False, num_devices=1)
    arrays, ins = {}, {}
    given = {name: inputs[name] for name in NAMES}
    given.update(constants())
    for name, a in given.items():
        a = np.ascontiguousarray(a)
        arrays["in_" + name] = a
        ins[name] = nc.dram_tensor("in_" + name, a.shape, mybir.dt.from_np(a.dtype), kind="ExternalInput").ap()
    out = nc.dram_tensor("out_0", (1, S, D), F32, kind="ExternalOutput").ap()
    build(nc, ins, out)
    r = run_bass_kernel_spmd(nc, [arrays], core_ids=[0])
    return r.results[0]["out_0"]
```
